# Optimizing a Trainium2 kernel written in Bass

```python
import jax, jax.numpy as jnp
from jax import lax
import numpy as np

D_MODEL = 2048
BATCH = 1
SEQ = 256
DEPTH = 1

EPS = 1e-6
NSA_HEAD_DIM = 128
NSA_HEADS = D_MODEL // 256
NSA_KV_GROUPS = 2
NSA_HPG = NSA_HEADS // NSA_KV_GROUPS
NSA_WIDTH = NSA_HEADS * NSA_HEAD_DIM
NSA_KV_WIDTH = NSA_KV_GROUPS * NSA_HEAD_DIM
CMP_BLOCK = 32
CMP_STRIDE = 16
SLC_BLOCK = 64
SLC_TOPK = 16
WINDOW = 512
Q_BLOCK = 128
SEL_BIG = 1e6
RWKV_HEAD_DIM = 64
RWKV_HEADS = D_MODEL // 128
RWKV_WIDTH = RWKV_HEADS * RWKV_HEAD_DIM
W_RANK = 64
A_RANK = 64
G_RANK = 160
LNX_EPS = 64e-5
NSA_COLS = NSA_WIDTH + 6 * NSA_KV_WIDTH + 3 * NSA_HEADS
RWKV_COLS = 3 * RWKV_WIDTH + W_RANK + A_RANK + G_RANK
IN_COLS = NSA_COLS + RWKV_COLS
MIX_WIDTH = NSA_WIDTH + RWKV_WIDTH
MEM_TOKENS = 256
MEM_HEADS = 4
MEM_HEAD_DIM = D_MODEL // MEM_HEADS
N_GROUPS = 4
EXPERTS_PER_GROUP = 8
N_EXPERTS = N_GROUPS * EXPERTS_PER_GROUP
TOP_K_INNER = 2
EXPERT_FF = 256

kernel_name = "hymba_nsa_rwkv7_hiermoe_layer"

def rmsnorm(x, g):
    xf = x.astype(jnp.float32)
    y = xf * lax.rsqrt(jnp.mean(xf * xf, axis=-1, keepdims=True) + EPS)
    return (y * g.astype(jnp.float32)).astype(x.dtype)

def split_cols(z, sizes):
    offs = np.cumsum([0] + list(sizes))
    return [z[..., int(offs[i]):int(offs[i + 1])] for i in range(len(sizes))]

def token_shift(z):
    return jnp.pad(z, ((0, 0), (1, 0), (0, 0)))[:, :-1]

def masked_softmax(s, mask):
    s = jnp.where(mask, s.astype(jnp.float32), -1e30)
    m = jnp.max(s, axis=-1, keepdims=True)
    e = jnp.where(mask, jnp.exp(s - m), 0.0)
    return e / jnp.maximum(jnp.sum(e, axis=-1, keepdims=True), 1e-30)

def compress_kv(kv, pos, w1, w2):
    B, T, G, Dh = kv.shape
    n_cmp = (T - CMP_BLOCK) // CMP_STRIDE + 1
    idx = jnp.arange(n_cmp)[:, None] * CMP_STRIDE + jnp.arange(CMP_BLOCK)[None, :]
    blocks = kv[:, idx] + pos[None, None, :, None, :]
    blocks = jnp.transpose(blocks, (0, 1, 3, 2, 4)).reshape(B, n_cmp, G, CMP_BLOCK * Dh)
    return jax.nn.gelu(blocks @ w1) @ w2

def nsa_mixer(q, kc, vc, ks, vs, kw, vw, gate_logits,
              cmp_pos_k, cmp_w1_k, cmp_w2_k, cmp_pos_v, cmp_w1_v, cmp_w2_v):
    B, T, _ = q.shape
    G, P, Dh = NSA_KV_GROUPS, NSA_HPG, NSA_HEAD_DIM
    scale = Dh ** -0.5

    def kv4(t):
        return t.reshape(B, T, G, Dh)

    q = q.reshape(B, T, G, P, Dh)
    gates = jax.nn.sigmoid(gate_logits.reshape(B, T, 3, G, P))
    k_cmp = compress_kv(kv4(kc), cmp_pos_k, cmp_w1_k, cmp_w2_k)
    v_cmp = compress_kv(kv4(vc), cmp_pos_v, cmp_w1_v, cmp_w2_v)
    n_cmp = k_cmp.shape[1]
    cmp_start = jnp.arange(n_cmp) * CMP_STRIDE
    cmp_end = cmp_start + CMP_BLOCK - 1
    n_sel = T // SLC_BLOCK
    sel_start = jnp.arange(n_sel) * SLC_BLOCK
    overlap = (jnp.minimum(cmp_start[:, None] + CMP_BLOCK, sel_start[None, :] + SLC_BLOCK)
               - jnp.maximum(cmp_start[:, None], sel_start[None, :]))
    cmp_to_sel = jnp.clip(overlap, 0, None).astype(jnp.float32) / CMP_BLOCK
    top_n = min(SLC_TOPK, n_sel)
    k_blk = jnp.transpose(kv4(ks).reshape(B, n_sel, SLC_BLOCK, G, Dh), (0, 3, 1, 2, 4))
    v_blk = jnp.transpose(kv4(vs).reshape(B, n_sel, SLC_BLOCK, G, Dh), (0, 3, 1, 2, 4))
    pad = ((0, 0), (WINDOW, 0), (0, 0), (0, 0))
    k_win = jnp.pad(kv4(kw), pad)
    v_win = jnp.pad(kv4(vw), pad)
    b_ix = jnp.arange(B)[:, None, None, None]
    g_ix = jnp.arange(G)[None, None, :, None]
    sel_j = jnp.arange(n_sel)
    slc_off = jnp.arange(SLC_BLOCK)
    win_off = jnp.arange(WINDOW + Q_BLOCK) - WINDOW

    def query_block(qi):
        q0 = qi * Q_BLOCK
        qpos = q0 + jnp.arange(Q_BLOCK)
        qb = lax.dynamic_slice_in_dim(q, q0, Q_BLOCK, axis=1)
        gb = lax.dynamic_slice_in_dim(gates, q0, Q_BLOCK, axis=1)
        s_c = jnp.einsum("bqgpd,bcgd->bqgpc", qb, k_cmp) * scale
        p_c = masked_softmax(s_c, (cmp_end[None, :] <= qpos[:, None])[None, :, None, None, :])
        o_c = jnp.einsum("bqgpc,bcgd->bqgpd", p_c.astype(v_cmp.dtype), v_cmp)
        p_sel = jnp.einsum("bqgpc,cs->bqgs", p_c, cmp_to_sel)
        blk = qpos // SLC_BLOCK
        forced = ((sel_j[None, :] == 0) | (sel_j[None, :] == blk[:, None])
                  | (sel_j[None, :] == blk[:, None] - 1))
        future = sel_j[None, :] > blk[:, None]
        score = jnp.where(future[None, :, None, :], -SEL_BIG,
                          p_sel + SEL_BIG * forced[None, :, None, :].astype(jnp.float32))
        _, sel_idx = lax.top_k(score, top_n)
        k_s = k_blk[b_ix, g_ix, sel_idx].reshape(B, Q_BLOCK, G, top_n * SLC_BLOCK, Dh)
        v_s = v_blk[b_ix, g_ix, sel_idx].reshape(B, Q_BLOCK, G, top_n * SLC_BLOCK, Dh)
        kpos_s = (sel_idx[..., None] * SLC_BLOCK + slc_off).reshape(B, Q_BLOCK, G, top_n * SLC_BLOCK)
        s_s = jnp.einsum("bqgpd,bqgnd->bqgpn", qb, k_s) * scale
        p_s = masked_softmax(s_s, (kpos_s <= qpos[None, :, None, None])[:, :, :, None, :])
        o_s = jnp.einsum("bqgpn,bqgnd->bqgpd", p_s.astype(v_s.dtype), v_s)
        k_w = lax.dynamic_slice_in_dim(k_win, q0, WINDOW + Q_BLOCK, axis=1)
        v_w = lax.dynamic_slice_in_dim(v_win, q0, WINDOW + Q_BLOCK, axis=1)
        kpos_w = q0 + win_off
        diff = qpos[:, None] - kpos_w[None, :]
        mask_w = (diff >= 0) & (diff < WINDOW) & (kpos_w[None, :] >= 0)
        s_w = jnp.einsum("bqgpd,bkgd->bqgpk", qb, k_w) * scale
        p_w = masked_softmax(s_w, mask_w[None, :, None, None, :])
        o_w = jnp.einsum("bqgpk,bkgd->bqgpd", p_w.astype(v_w.dtype), v_w)
        o = (gb[:, :, 0, :, :, None] * o_c + gb[:, :, 1, :, :, None] * o_s
             + gb[:, :, 2, :, :, None] * o_w)
        return o.reshape(B, Q_BLOCK, NSA_WIDTH)

    out = lax.map(query_block, jnp.arange(T // Q_BLOCK))
    return jnp.transpose(out, (1, 0, 2, 3)).reshape(B, T, NSA_WIDTH)

def rwkv7_scan(r, w, k, v, kk, a):
    B, T, H, N = r.shape

    def step(S, inp):
        r_t, w_t, k_t, v_t, kk_t, a_t = inp
        sa = jnp.einsum("bhij,bhj->bhi", S, -kk_t)
        S = (S * w_t[:, :, None, :] + sa[..., None] * (kk_t * a_t)[:, :, None, :]
             + v_t[..., None] * k_t[:, :, None, :])
        return S, jnp.einsum("bhij,bhj->bhi", S, r_t)

    xs = tuple(jnp.moveaxis(t.astype(jnp.float32), 1, 0) for t in (r, w, k, v, kk, a))
    _, y = lax.scan(step, jnp.zeros((B, H, N, N), jnp.float32), xs)
    return jnp.moveaxis(y, 0, 1)

def rwkv7_mixer(z, mu, w0, w_up, a0, a_up, g_up, k_k, k_a, r_k, lnx_g, lnx_b):
    B, T, _ = z.shape
    z = z + (token_shift(z) - z) * mu
    r, k, v, wd, ad, gd = split_cols(z, [RWKV_WIDTH] * 3 + [W_RANK, A_RANK, G_RANK])
    w_log = -jax.nn.softplus(-(w0 + jnp.tanh(wd) @ w_up)) - 0.5
    decay = jnp.exp(-jnp.exp(w_log.astype(jnp.float32)))
    a = jax.nn.sigmoid(a0 + ad @ a_up)
    g = jax.nn.sigmoid(gd) @ g_up

    def heads(t):
        return t.reshape(B, T, RWKV_HEADS, RWKV_HEAD_DIM)

    kk = heads(k * k_k).astype(jnp.float32)
    kk = kk * lax.rsqrt(jnp.maximum(jnp.sum(kk * kk, axis=-1, keepdims=True), 1e-24))
    k = k * (1.0 + (a - 1.0) * k_a)
    r_h, k_h, v_h = heads(r), heads(k), heads(v)
    y = rwkv7_scan(r_h, heads(decay), k_h, v_h, kk, heads(a))
    mean = jnp.mean(y, axis=-1, keepdims=True)
    var = jnp.mean(jnp.square(y - mean), axis=-1, keepdims=True)
    y = ((y - mean) * lax.rsqrt(var + LNX_EPS)).reshape(B, T, RWKV_WIDTH) * lnx_g + lnx_b
    bonus = jnp.sum(r_h * k_h * r_k, axis=-1, keepdims=True) * v_h
    y = y + bonus.reshape(B, T, RWKV_WIDTH)
    return (y * g).astype(z.dtype)

def memory_attention(h, m, wq, wk, wv, wo):
    B, T, _ = h.shape
    M = m.shape[1]
    q = (h @ wq).reshape(B, T, MEM_HEADS, MEM_HEAD_DIM)
    k = (m @ wk).reshape(B, M, MEM_HEADS, MEM_HEAD_DIM)
    v = (m @ wv).reshape(B, M, MEM_HEADS, MEM_HEAD_DIM)
    s = jnp.einsum("bthd,bmhd->bhtm", q, k).astype(jnp.float32) * MEM_HEAD_DIM ** -0.5
    p = jax.nn.softmax(s, axis=-1)
    o = jnp.einsum("bhtm,bmhd->bthd", p.astype(v.dtype), v).reshape(B, T, MEM_HEADS * MEM_HEAD_DIM)
    return o @ wo

def hier_moe(h, wg_r, bg_r, we_r, be_r, w_gate, w_up, w_down):
    B, T, D = h.shape
    hf = h.reshape(B * T, D)
    n = hf.shape[0]
    p_group = jax.nn.softmax((hf @ wg_r + bg_r).astype(jnp.float32), axis=-1)
    pg_top, g_idx = lax.top_k(p_group, 1)
    e_logits = (hf @ we_r + be_r).reshape(n, N_GROUPS, EXPERTS_PER_GROUP)
    e_logits = jnp.take_along_axis(e_logits, g_idx[:, :, None], axis=1)[:, 0]
    p_exp = jax.nn.softmax(e_logits.astype(jnp.float32), axis=-1)
    pe_top, e_idx = lax.top_k(p_exp, TOP_K_INNER)
    wts = pg_top * pe_top / jnp.sum(pe_top, axis=-1, keepdims=True)
    flat = g_idx * EXPERTS_PER_GROUP + e_idx
    combine = jnp.sum(jax.nn.one_hot(flat, N_EXPERTS, dtype=jnp.float32) * wts[..., None],
                      axis=1).astype(h.dtype)
    y = jnp.zeros_like(hf)
    for grp in range(N_GROUPS):
        sl = slice(grp * EXPERTS_PER_GROUP, (grp + 1) * EXPERTS_PER_GROUP)
        hid = (jax.nn.silu(jnp.einsum("nd,edf->nef", hf, w_gate[sl]))
               * jnp.einsum("nd,edf->nef", hf, w_up[sl]))
        y = y + jnp.einsum("nef,efd->nd", hid * combine[:, sl, None], w_down[sl])
    return y.reshape(B, T, D)

def setup_inputs(seed: int = 0) -> dict:
    key = jax.random.key(seed)
    keys = iter(jax.random.split(key, 64))
    L = DEPTH

    def nrm(shape, scale):
        return jax.random.normal(next(keys), shape, jnp.float32) * scale

    def unif(shape, lo, hi):
        return jax.random.uniform(next(keys), shape, jnp.float32, lo, hi)

    def gain(n):
        return 1.0 + nrm((L, n), 0.02)

    return {
        "x": nrm((BATCH, SEQ, D_MODEL), 1.0),
        "mem": nrm((BATCH, MEM_TOKENS, D_MODEL), 1.0),
        "ln1_g": gain(D_MODEL),
        "w_in": nrm((L, D_MODEL, IN_COLS), D_MODEL ** -0.5),
        "cmp_pos_k": nrm((L, CMP_BLOCK, NSA_HEAD_DIM), 0.02),
        "cmp_w1_k": nrm((L, CMP_BLOCK * NSA_HEAD_DIM, NSA_HEAD_DIM), (CMP_BLOCK * NSA_HEAD_DIM) ** -0.5),
        "cmp_w2_k": nrm((L, NSA_HEAD_DIM, NSA_HEAD_DIM), NSA_HEAD_DIM ** -0.5),
        "cmp_pos_v": nrm((L, CMP_BLOCK, NSA_HEAD_DIM), 0.02),
        "cmp_w1_v": nrm((L, CMP_BLOCK * NSA_HEAD_DIM, NSA_HEAD_DIM), (CMP_BLOCK * NSA_HEAD_DIM) ** -0.5),
        "cmp_w2_v": nrm((L, NSA_HEAD_DIM, NSA_HEAD_DIM), NSA_HEAD_DIM ** -0.5),
        "nsa_norm_g": gain(NSA_WIDTH),
        "rwkv_mu": unif((L, RWKV_COLS), 0.0, 1.0),
        "rwkv_w0": unif((L, RWKV_WIDTH), -5.0, 1.0),
        "rwkv_w_up": nrm((L, W_RANK, RWKV_WIDTH), 0.5 * W_RANK ** -0.5),
        "rwkv_a0": nrm((L, RWKV_WIDTH), 0.1),
        "rwkv_a_up": nrm((L, A_RANK, RWKV_WIDTH), 0.5 * A_RANK ** -0.5),
        "rwkv_g_up": nrm((L, G_RANK, RWKV_WIDTH), G_RANK ** -0.5),
        "rwkv_k_k": 0.85 + nrm((L, RWKV_WIDTH), 0.02),
        "rwkv_k_a": 1.0 + nrm((L, RWKV_WIDTH), 0.02),
        "rwkv_r_k": nrm((L, RWKV_HEADS, RWKV_HEAD_DIM), 0.1),
        "rwkv_lnx_g": gain(RWKV_WIDTH),
        "rwkv_lnx_b": nrm((L, RWKV_WIDTH), 0.01),
        "w_out": nrm((L, MIX_WIDTH, D_MODEL), MIX_WIDTH ** -0.5),
        "ln_mem_g": gain(D_MODEL),
        "ln2_g": gain(D_MODEL),
        "wq_mem": nrm((L, D_MODEL, MEM_HEADS * MEM_HEAD_DIM), D_MODEL ** -0.5),
        "wk_mem": nrm((L, D_MODEL, MEM_HEADS * MEM_HEAD_DIM), D_MODEL ** -0.5),
        "wv_mem": nrm((L, D_MODEL, MEM_HEADS * MEM_HEAD_DIM), D_MODEL ** -0.5),
        "wo_mem": nrm((L, MEM_HEADS * MEM_HEAD_DIM, D_MODEL), (MEM_HEADS * MEM_HEAD_DIM) ** -0.5),
        "ln3_g": gain(D_MODEL),
        "router_group_w": nrm((L, D_MODEL, N_GROUPS), D_MODEL ** -0.5),
        "router_group_b": nrm((L, N_GROUPS), 0.01),
        "router_expert_w": nrm((L, D_MODEL, N_EXPERTS), D_MODEL ** -0.5),
        "router_expert_b": nrm((L, N_EXPERTS), 0.01),
        "moe_w_gate": nrm((L, N_EXPERTS, D_MODEL, EXPERT_FF), D_MODEL ** -0.5),
        "moe_w_up": nrm((L, N_EXPERTS, D_MODEL, EXPERT_FF), D_MODEL ** -0.5),
        "moe_w_down": nrm((L, N_EXPERTS, EXPERT_FF, D_MODEL), EXPERT_FF ** -0.5),
        "lnf_g": 1.0 + nrm((D_MODEL,), 0.02),
    }

def reference(x, mem, ln1_g, w_in, cmp_pos_k, cmp_w1_k, cmp_w2_k, cmp_pos_v, cmp_w1_v, cmp_w2_v,
              nsa_norm_g, rwkv_mu, rwkv_w0, rwkv_w_up, rwkv_a0, rwkv_a_up, rwkv_g_up, rwkv_k_k,
              rwkv_k_a, rwkv_r_k, rwkv_lnx_g, rwkv_lnx_b, w_out, ln_mem_g, ln2_g, wq_mem, wk_mem,
              wv_mem, wo_mem, ln3_g, router_group_w, router_group_b, router_expert_w,
              router_expert_b, moe_w_gate, moe_w_up, moe_w_down, lnf_g):
    for l in range(DEPTH):
        h = rmsnorm(x, ln1_g[l])
        z = h @ w_in[l]
        z_nsa, z_rwkv = z[..., :NSA_COLS], z[..., NSA_COLS:]
        q, kc, vc, ks, vs, kw, vw, gl = split_cols(
            z_nsa, [NSA_WIDTH] + [NSA_KV_WIDTH] * 6 + [3 * NSA_HEADS])
        y_a = nsa_mixer(q, kc, vc, ks, vs, kw, vw, gl, cmp_pos_k[l], cmp_w1_k[l], cmp_w2_k[l],
                        cmp_pos_v[l], cmp_w1_v[l], cmp_w2_v[l])
        y_a = rmsnorm(y_a, nsa_norm_g[l])
        y_b = rwkv7_mixer(z_rwkv, rwkv_mu[l], rwkv_w0[l], rwkv_w_up[l], rwkv_a0[l], rwkv_a_up[l],
                          rwkv_g_up[l], rwkv_k_k[l], rwkv_k_a[l], rwkv_r_k[l], rwkv_lnx_g[l],
                          rwkv_lnx_b[l])
        x = x + jnp.concatenate([y_a.astype(x.dtype), y_b.astype(x.dtype)], axis=-1) @ w_out[l]
        x = x + memory_attention(rmsnorm(x, ln2_g[l]), rmsnorm(mem, ln_mem_g[l]),
                                 wq_mem[l], wk_mem[l], wv_mem[l], wo_mem[l])
        x = x + hier_moe(rmsnorm(x, ln3_g[l]), router_group_w[l], router_group_b[l],
                         router_expert_w[l], router_expert_b[l], moe_w_gate[l], moe_w_up[l],
                         moe_w_down[l])
    return rmsnorm(x, lnf_g)


_drawn_inputs = setup_inputs


def setup_inputs(seed=0):
    import zlib

    import numpy as np

    out = dict(_drawn_inputs(seed))
    spreads = {}
    factors = {'cmp_pos_k': 5.846,
     'nsa_norm_g': 3.113,
     'rwkv_w_up': 3.149,
     'rwkv_k_k': 3.806,
     'rwkv_k_a': 4.484,
     'rwkv_lnx_g': 4.46,
     'rwkv_lnx_b': 8.0,
     'ln_mem_g': 8.0,
     'ln2_g': 8.0,
     'router_group_b': 31.008,
     'router_expert_b': 43.216,
     'lnf_g': 8.157,
     'ln3_g': 8.0}
    for name, (base, spread) in spreads.items():
        noise = np.random.default_rng([zlib.crc32(name.encode()), seed]).standard_normal(out[name].shape)
        drawn = base * np.exp(spread * noise) if base else spread * noise
        out[name] = __import__('jax').numpy.asarray(drawn.astype(out[name].dtype))
    for name, factor in factors.items():
        out[name] = (out[name] * factor).astype(out[name].dtype)
    return out
```

```python
from contextlib import ExitStack

import concourse.bass as bass
from concourse import mybir

F32 = mybir.dt.float32
F32R = mybir.dt.float32r
I32 = mybir.dt.int32
ALU = mybir.AluOpType
ACT = mybir.ActivationFunctionType
AX = mybir.AxisListType

P = 128
T, D = 256, 2048
NT = T // P
NC = D // P
EPS = 1e-6
HD = 128
NH, NG = 8, 2
CMP, STRIDE = 32, 16
NCMP = (T - CMP) // STRIDE + 1
KAPPA = 0.6065306597126334
LNX_EPS = 64e-5
CH = 64
NCH = T // CH
NGRP = 4
NSA_COLS = 2584
RW = 1024
MH, MHD = 4, 512
NGR, EPG, NE, FF = 4, 8, 32, 256
CAP = P
UC = 256
RING = 4
MRAW = 3
SPLITS = 3
DSHARE = 1536
BIG = -1e30


class Progress:

    def __init__(self, sem, steps):
        self.sem, self.steps, self.n = sem, list(steps), 0
        self.value = {k: i + 1 for i, k in enumerate(self.steps)}
        assert len(self.value) == len(self.steps)

    def at(self, key):
        return self.sem, self.value[key]

    def mark(self, key):
        assert self.steps[self.n] == key, (self.steps[self.n], key)
        self.n += 1
        return self.sem, 1


def decoder_layer(nc, x_in, mem, ln1_g, w_in, cmp_pos_k, cmp_w1_k, cmp_w2_k, cmp_pos_v, cmp_w1_v,
                  cmp_w2_v, nsa_norm_g, rwkv_mu, rwkv_w0, rwkv_w_up, rwkv_a0, rwkv_a_up, rwkv_g_up,
                  rwkv_k_k, rwkv_k_a, rwkv_r_k, rwkv_lnx_g, rwkv_lnx_b, w_out, ln_mem_g, ln2_g,
                  wq_mem, wk_mem, wv_mem, wo_mem, ln3_g, router_group_w, router_group_b,
                  router_expert_w, router_expert_b, moe_w_gate, moe_w_up, moe_w_down, lnf_g, out):
    ctx = ExitStack()
    with ctx:
        def sem(name):
            return ctx.enter_context(nc.semaphore(name))

        ARENA = 52992
        FIXED = 25280
        arenas = [ctx.enter_context(nc.sbuf_tensor("arena_fixed", [P, FIXED], F32)),
                  ctx.enter_context(nc.sbuf_tensor("arena_phases", [P, ARENA - FIXED], F32))]
        arena_base = nc.sbuf_base - 4 * ARENA

        def over(name, at, *dims, dtype=F32R):
            return nc.alloc_sbuf_tensor_at(name, [P, *dims], dtype, offset=arena_base + 4 * at)

        small_i = ctx.enter_context(nc.sbuf_tensor("small_i", [P, 128], I32))

        class Region:
            def __init__(self, start, end):
                self.at, self.end = start, end

            def take(self, *dims):
                n = 1
                for d in dims:
                    n *= d
                assert self.at + n <= self.end, (self.at, n, self.end)
                k = int(self.at >= FIXED)
                assert k or self.at + n <= FIXED
                v = arenas[k][:, self.at - k * FIXED:self.at + n - k * FIXED]
                self.at += n
                if len(dims) == 1:
                    return v
                names = "abcde"[:len(dims)]
                kw = {c: d for c, d in zip(names[1:], dims[1:])}
                return v.rearrange(f"p ({' '.join(names)}) -> p {' '.join(names)}", **kw)

        UN = NC * UC
        fixed = Region(0, FIXED)
        ring = fixed.take(RING, UN)
        hT_at = fixed.at
        hT = fixed.take(NC, T)
        concat_at = fixed.at
        concatT = fixed.take(NC, T)
        ident = fixed.take(P)
        bd64 = fixed.take(P)
        prm = fixed.take(2 * P)
        prm2 = fixed.take(25)
        hm = fixed.take(4)
        rms_s = fixed.take(2)
        rms_r = fixed.take(2)
        gates = fixed.take(2, 24)
        maskc = fixed.take(2, 16)
        biasc = fixed.take(2, 16)
        start = FIXED
        MEM_SLOT = 3
        x_slot = ring[:, 0, :].rearrange("p (t d) -> p t d", t=NT)

        r1 = Region(start, ARENA)
        qT = r1.take(NH, T)
        kvc = r1.take(4, T)
        ksw = r1.take(4, T)
        vsw = r1.take(2, NT, 256)
        nsa_end = r1.at
        M2 = r1.take(2, P)
        MTk = r1.take(6, P)
        M0 = r1.take(P)
        reset = r1.take(T)
        zraw = r1.take(6, T + 1)
        z = r1.take(6, T)
        wad = r1.take(2, T)
        gds = r1.take(2, T)
        wup = r1.take(256)
        aup = r1.take(256)
        gup = r1.take(2, 256)
        tA, tB, tC, tD, tE, tF, tG, tH, tI = (r1.take(2, T) for _ in range(9))
        fac = r1.take(2, 4)
        em = r1.take(2, 4)
        CR = r1.take(2, 2, 2, T)
        BK = r1.take(2, 2, T)
        BKt = r1.take(2, 2, 2, P)
        Vh = r1.take(2, 2, 2, P)
        AK = r1.take(2, 4, 2, P)
        AB = r1.take(2, 4, 2, P)
        XI = concatT[:, 0:4, :].rearrange("p (a b) (c d) -> p a (b c) d", a=2, c=2)
        XT = concatT[:, 4:8, :].rearrange("p (a b) (c d) -> p a (b c) d", a=2, c=2)
        AM = r1.take(2, 4, P)
        Ps = BK.rearrange("p a b (c d) -> p a (b c) d", c=2)
        S = r1.take(2, 2, CH)
        Zs = r1.take(4, CH)
        Us = r1.take(4, CH)

        r2 = Region(nsa_end, ARENA)
        kmT = r2.take(NC, T)
        vm = r2.take(NT, D)
        keep2 = r2.at
        biasw = r2.take(2, T)
        blk = r2.take(2, CMP, 2 * NCMP)
        hc = r2.take(2, 32)
        hc2 = r2.take(2, 32)
        hc3 = r2.take(2, 32)
        w2 = r2.take(2, P)
        kcmp = r2.take(32)
        vcmp = r2.take(2, P)
        sm = r2.take(2, 2 * T + 16)
        pr = r2.take(2, 2 * T + 16)
        pT = r2.take(2, 5, P)
        ya = r2.take(NT, NH * HD)
        mxs = r2.take(2, 4)
        sums = r2.take(2, 4)
        coef = r2.take(2, 4)

        mem_slot = ring[:, MEM_SLOT, :].rearrange("p (t d) -> p t d", t=NT)

        r3 = Region(keep2, ARENA)
        r3b = Region(start, ARENA)
        xn = r3b.take(NT, D)
        assert r3b.at <= nsa_end
        x = r3.take(NT, D)
        x_end = r3.at
        mp = r3.take(2, T)
        mpT = r3.take(2, 2, T)
        mst = r3.take(2, 8)
        oT = concatT
        qmT = xn.rearrange("p t d -> p (t d)").rearrange("p (c t) -> p c t", t=T)

        HU = UN // 2
        spl = [over(f"split{i}", at, 2, HU) for i, at in
               enumerate((MRAW * UN, nsa_end, nsa_end + UN))]
        assert nsa_end + 2 * UN <= keep2
        raw = over("weights_raw", 0, MRAW, UN, dtype=F32)
        h3 = (over("h3_hi", concat_at, NT, D), over("h3_lo", start, NT, D))
        hs = (over("gathered_hi", hT_at, NC, P), over("gathered_lo", hT_at + NC * P, NC, P))
        r5 = Region(r3.at, ARENA)
        late = Region(nsa_end, keep2)
        lnb, rw, rb = late.take(D), late.take(NC, 36), late.take(36)
        r5.at = -(-r5.at // 8) * 8

        def take_over(name, *dims):
            v = over(name, r5.at, *dims)
            r5.take(*dims)
            return v

        osp = [take_over(f"down_hi_lo_{i}", 2, 512) for i in range(2)]
        hid = r5.take(FF)
        thm = r5.take(FF)
        tTs = (take_over("hidden_hi", 2, P), take_over("hidden_lo", 2, P))
        G = take_over("gather_onehots", NT, P)
        Gt = take_over("scatter_onehots", NT, P)
        wcol, wc1 = r5.take(EPG), r5.take(1)
        assert r3.at <= ARENA - 2 * UN
        lspl = [over(f"loop_split{i}", at, 2, HU) for i, at in
                enumerate((2 * UN, 3 * UN, ARENA - 2 * UN, ARENA - UN))]
        over_hT, over_concat = over("act_over_hT", hT_at, NC, T), over("act_over_concat", concat_at, NC, T)
        lnf = ring[:, 0, 0:D]
        pcol, ccol = r5.take(2, 1), r5.take(2, EPG)
        iota_r = r5.take(CAP)
        strictU = r5.take(P)
        ones = r5.take(P)
        lg = r5.take(2, 36)
        gd_, ge, geq, goh = (r5.take(2, NGR) for _ in range(4))
        rmax, rtop, pg, m2, e2, w1_, w2_ = (r5.take(2) for _ in range(7))
        d8, eq8, o1, o2, c8 = (r5.take(2, EPG) for _ in range(5))
        rtmp = r5.take(2, NE)
        comb = r5.take(2, NE + EPG)
        posm = r5.take(2, NGR + 1)
        wtie = r5.take(EPG)
        otmp = r5.take(4)
        otick = r5.take(8)
        oflag, kval, otmp4 = (r5.take(NGR) for _ in range(3))
        osum = r5.take(3)
        ioti = small_i[:, 0:P]
        count_i = ctx.enter_context(nc.sbuf_tensor("visit_counts", [P, 4], I32))

        def slot(s):
            return ring[:, s, :]

        def unit_kc(s):
            return slot(s).rearrange("p (c n) -> p c n", n=UC)

        c_ln1, c_lnm, c_ln2, c_nsa, c_w0, c_a0, c_kk, c_ka, c_rk, c_lg, c_lb = (
            0, 16, 32, 48, 56, 64, 72, 80, 88, 96, 104)
        c_mu, c_posk, c_posv = 128, 156, 188

        def col(i):
            return prm[:, i:i + 1]

        bank = [ctx.enter_context(nc.psum_tensor(f"bank{i}", [P, 512], F32)) for i in range(8)]

        def b2(i, n=2):
            return bank[i][:, :].rearrange("p (a b) -> p a b", a=n)

        win = w_in[0].rearrange("(c p) n -> p c n", p=P)
        R0 = NSA_COLS
        units = []

        def wcols(w, c0):
            return w[:, :, c0:c0 + UC]

        units.append(("x", "x", 0))
        units.append(("misc", win, R0 + 3 * RW))
        units.append(("misc2", win, None))

        def rkv(g):
            for j in range(3):
                units.append((("rkv", g, j), win, R0 + j * RW + g * UC))

        rkv(0)
        nsa_order = [[("q", 0), ("q", 1)], [("q", 2), ("q", 3)], [("kc", 0), ("vc", 0)],
                     [("ks", 0), ("kw", 0), ("vs", 0), ("vw", 0)]]
        nsa_col = {("q", i): 256 * i for i in range(4)}
        nsa_col.update({("kc", 0): 1024, ("vc", 0): 1280, ("ks", 0): 1536, ("vs", 0): 1792,
                        ("kw", 0): 2048, ("vw", 0): 2304})
        fill_of = []
        for g in range(NGRP):
            first = len(units)
            for key in nsa_order[g]:
                units.append((key, win, nsa_col[key]))
            if g + 1 < NGRP:
                rkv(g + 1)
            fill_of.append(list(range(first, len(units))))
        units.append(("w1k", "w1", 0))
        units.append(("w1v", "w1", 1))
        units.append(("mem", "mem", 0))
        wkm = wk_mem[0].rearrange("(c p) n -> p c n", p=P)
        wvm = wv_mem[0].rearrange("(c p) n -> p c n", p=P)
        mem_first = len(units)
        for i in range(8):
            units.append((("mk", i), wkm, i * UC))
        for i in range(8):
            units.append((("mv", i), wvm, i * UC))
        mem_units = list(range(mem_first, len(units)))
        while len(units) % RING:
            units.append(("pad", None, 0))
        loop_first = len(units)
        index = {k: i for i, (k, _, _) in enumerate(units)}
        LOOPS = (("wout", w_out[0]), ("wq", wq_mem[0]), ("wo", wo_mem[0]))
        NLU = D // UC
        n_before = loop_first + NLU * len(LOOPS)
        assert index["mem"] % RING == MEM_SLOT
        NLT = NLU * len(LOOPS)
        assert NLU % 2 == 0

        ring_full = [sem(f"ring_full{s}") for s in range(RING)]
        moe_full = [sem(f"moe_raw_full{s}") for s in range(MRAW)]

        def full(u):
            return ring_full[u % RING], 16 * (u // RING + 1)

        s_prm = sem("params_loaded")
        s_up = sem("up_loaded")
        s_gl = [sem("wd_ad_loaded"), sem("gate_weights_loaded")]
        s_w2 = sem("w2_loaded")
        s_x = sem("x_loaded")
        s_late = sem("late_params_loaded")
        s_out = sem("out_stored")
        dve_self, act_self, pool_self = sem("dve_self"), sem("act_self"), sem("pool_self")

        class Chain:

            def __init__(self, eng, s):
                self.eng, self.s, self.n = eng, s, 0

            def __call__(self, ins):
                self.n += 1
                ins.then_inc(self.s, 1)
                self.eng.wait_ge(self.s, self.n)

        proj = [i for i, (k, _, _) in enumerate(units) if k not in ("x", "mem", "w1k", "w1v", "pad")]
        order = {u: n for n, u in enumerate(proj)}
        last_in = [u for u in proj if u < index["w1k"]][-1]
        TOKMAJOR = {("vs", 0), ("vw", 0)} | {("mv", i) for i in range(8)}
        pe_proj = Progress(sem("pe_projected"), proj)
        act_proj = Progress(sem("act_projection_copied"), proj)

        pool_c = Progress(sem("pool_constants"), ["clear", "ident", "masks", "nsa", "moe"])
        pe_c = Progress(sem("pe_params"), ["prm"])
        dve_c = Progress(sem("dve_params"), ["prm", "mixm", "gds"])
        act_c = Progress(sem("act_params"), ["tm"])

        LV = range(1, 6)
        pe_rw = Progress(sem("pe_rwkv"), [
            k for g in range(NGRP) for k in
            [("wa", g), ("ss", g), ("bon", g), ("tr", g), ("G", g, 0), ("G", g, 1)]
            + [k for lv in LV for k in [("P", g, lv, 0), ("P", g, lv, 1), ("X", g, lv, 0), ("X", g, lv, 1)]]
            + [k for c in range(NCH) for k in [("Z", g, c), ("U", g, c), ("Y", g, c)]]
            + [("mean", g), ("g", g)]])
        act_rw = Progress(sem("act_rwkv"), [
            k for g in range(NGRP) for k in
            [("th", g), ("exp", g), ("sq1", g), ("trb", g)]
            + [("Ps", g, lv, tt) for lv in LV for tt in range(2)]
            + [("Zs", g, c) for c in range(NCH)] + [("ys", g), ("sq2", g)]])
        dve_rw = Progress(sem("dve_rwkv"), [
            k for g in range(NGRP) for k in
            [("mix", g), ("kx2", g), ("D", g), ("ssm", g), ("bon", g), ("hat", g), ("Vh", g), ("G", g, 0),
             ("G", g, 1)]
            + [("X", g, lv, tt) for lv in LV for tt in range(2)]
            + [k for c in range(NCH) for k in
               ([("Us", g, c), ("S", g, c)] if c < NCH - 1 else [("Us", g, c)])]
            + [("yc", g), ("ve", g), ("out", g)]])
        pool_rw = Progress(sem("pool_rwkv"), [
            k for g in range(NGRP) for k in
            [("X0", g, 0), ("X0", g, 1)] + [("AM", g, lv, tt) for lv in LV for tt in range(2)]])

        NORMS = ("n1", "nm", "na", "n2", "n3")
        fills = {k: (4 if k == "na" else 8) for k in NORMS}
        act_n = Progress(sem("act_norm"), [k for n in NORMS + ("nf",) for k in [(n, "sq"), (n, "sqrt")]])
        dve_n = Progress(sem("dve_norm"), [k for n in NORMS for k in
                                           [(n, "var"), (n, "xn")] + [(n, "out", f) for f in range(fills[n])]]
                         + [("nf", "var"), ("nf", "out")])
        pe_n = Progress(sem("pe_norm"), [(n, f) for n in NORMS for f in range(fills[n])])

        HT = [(h, tt) for h in range(NH) for tt in range(NT)]
        NHT = len(HT)
        pe_a = Progress(sem("pe_nsa"), ["h", "kv"] + [
            k for i in range(NHT + 2) for k in
            ([("s", i)] if i < NHT else []) + ([("t", i - 1)] if 0 < i <= NHT else [])
            + ([("o", i - 2)] if i > 1 else [])])
        dve_a = Progress(sem("dve_nsa"), ["cube", "gelu", "kcmp"] + [
            k for i in range(NHT + 1) for k in
            ([("m", i)] if i < NHT else []) + ([("p", i - 1)] if i > 0 else [])])
        act_a = Progress(sem("act_nsa"), ["hc", "th"] + [
            k for i in range(NHT + 2) for k in
            ([("e", i)] if i < NHT else []) + ([("t", i - 1)] if 0 < i <= NHT else [])
            + ([("o", i - 2)] if i > 1 else [])])
        pool_a = Progress(sem("pool_nsa"), ["blk"])

        pe_loop = sem("pe_loop")
        loop_full = [sem(f"loop_raw_full{i}") for i in range(2)]
        loop_hi, loop_lo, loop_lo_pool = sem("loop_hi"), sem("loop_lo_dve"), sem("loop_lo_pool")
        src_hi, src_lo = sem("loop_activations_hi"), sem("loop_activations_lo")
        out_loop = sem("loop_copied")

        pe_m = Progress(sem("pe_mem"), [k for h in range(MH) for k in
                                        [("s", h, 0), ("s", h, 1), ("t", h), ("o", h)]])
        dve_m = Progress(sem("dve_mem"), [k for h in range(MH) for k in
                                          [("m", h, 0), ("m", h, 1), ("p", h, 0), ("p", h, 1)]])
        act_m = Progress(sem("act_mem"), [k for h in range(MH) for k in
                                          [("e", h, 0), ("e", h, 1), ("t", h), ("o", h)]])

        pe_r = Progress(sem("pe_router"), ["logits", "pos", "cnt"])
        dve_r = Progress(sem("dve_router"), ["h3lo", "gd", "m2", "routed", "posm", "most", "ovi"])
        act_r = Progress(sem("act_router"), ["h3hi", "ge", "e2"])

        act_hi, dve_lo, pool_lo = sem("moe_weights_hi"), sem("moe_weights_lo_dve"), sem("moe_weights_lo_pool")
        pe_hu = sem("moe_half_units_read")
        BH = 6

        def half_unit(E, off):
            return off if E is None else BH * E + 4 + off

        def loads_of(E, off):
            return 1 if E is None else E + (2 if off < 4 else 1)

        pe_cm = sem("moe_weights_gathered")
        pe_hs, act_hs, dve_hs = sem("moe_gathered"), sem("moe_gathered_hi"), sem("moe_gathered_lo")
        act_th, dve_h1, dve_hid = sem("moe_tanh"), sem("moe_hidden_1"), sem("moe_hidden")
        pe_gt, dve_gt = sem("moe_onehots_transposed"), sem("moe_onehots_copied")
        pe_trh, act_tT, dve_tT = sem("moe_hidden_transposed"), sem("moe_hidden_hi"), sem("moe_hidden_lo")
        act_os, dve_os = sem("moe_down_hi"), sem("moe_down_lo")
        pe_sc, dve_sc = sem("moe_scattered"), sem("moe_added")
        pool_g, pool_mc = sem("moe_gather_onehot"), sem("moe_columns")

        def freed(u):
            key = units[u][0]
            if key == "x":
                return pe_n.at(("n1", 7))
            if key == "mem":
                return pe_n.at(("nm", 7))
            if key in ("w1k", "w1v"):
                return pe_a.at("h")
            return pe_proj.at(u)

        FILLS = [26, 4, 4, 4, 3, 3] + [2] * 20 + [2] * 12 + [4]
        FILL2 = 11

        def bc(ap, *shape):
            return ap.broadcast_to([ap.shape[0], *shape])

        def flat(ap):
            return ap.rearrange("p a b -> p (a b)")

        block = ctx.enter_context(nc.Block())

        @block.sync
        def _(sp):
            def load(u):
                key, src, c0 = units[u]
                if key == "pad":
                    return
                if u >= RING and units[u - RING][0] != "pad":
                    sp.wait_ge(*freed(u - RING))
                s = u % RING
                dst = unit_kc(s)
                if key in ("x", "mem"):
                    src = (x_in if key == "x" else mem)[0].rearrange("(t p) d -> p t d", p=P)
                    dst = slot(s).rearrange("p (t d) -> p t d", t=NT)
                elif key in ("w1k", "w1v"):
                    w1 = (cmp_w1_k if key == "w1k" else cmp_w1_v)[0]
                    src = w1.rearrange("(l d) f -> d l f", d=HD)
                    dst = slot(s).rearrange("p (l f) -> p l f", l=CMP)
                elif key == "misc":
                    sp.dma_start(dst[:, :, P:2 * P], win[:, :, R0 + 3 * RW:R0 + 3 * RW + P]).then_inc(s_gl[0], 16)
                    src, dst = win[:, :, R0 + 3 * RW + P:R0 + 3 * RW + 2 * P], dst[:, :, 0:P]
                elif key == "misc2":
                    sp.dma_start(dst[:, :, 0:24], win[:, :, 2560:2584]).then_inc(s_gl[1], 16)
                    src, dst = win[:, :, R0 + 3 * RW + 256:R0 + 3 * RW + 288], dst[:, :, 32:64]
                else:
                    src = wcols(src, c0)
                sp.dma_start(dst, src).then_inc(ring_full[s], 16)

            load(0)
            sp.wait_ge(*pool_c.at("clear"))
            rows = ((ln1_g, 0, 16), (ln_mem_g, 16, 16), (ln2_g, 32, 16), (nsa_norm_g, 48, 8),
                    (rwkv_w0, 56, 8), (rwkv_a0, 64, 8), (rwkv_k_k, 72, 8), (rwkv_k_a, 80, 8),
                    (None, 88, 8), (rwkv_lnx_g, 96, 8), (rwkv_lnx_b, 104, 8))
            for w, r, n in rows:
                src = (rwkv_r_k[0].rearrange("(a b) d -> a (b d)", b=2) if w is None
                       else w[0].rearrange("(a b) -> a b", b=P))
                sp.dma_start(tA[r:r + n, 0, 0:P], src).then_inc(s_prm, 16)
            mu = rwkv_mu
            for r, n, c0, w in ((0, 24, 0, P), (24, 1, 3072, 64), (25, 1, 3136, 64), (26, 1, 3200, P),
                                (27, 1, 3328, 32)):
                sp.dma_start(tB[r:r + n, 0, 0:w], mu[0, c0:c0 + n * w].rearrange("(a b) -> a b", b=w))\
                  .then_inc(s_prm, 16)
            sp.dma_start(tB[28:60, 0, 0:P], cmp_pos_k[0]).then_inc(s_prm, 16)
            sp.dma_start(tB[60:92, 0, 0:P], cmp_pos_v[0]).then_inc(s_prm, 16)
            for u in range(1, RING):
                load(u)

            def load_up(g):
                if g:
                    sp.wait_ge(*pe_rw.at(("g", g - 1)))
                cs = slice(g * 256, g * 256 + 256)
                sp.dma_start(wup[0:64, :], rwkv_w_up[0, :, cs]).then_inc(s_up, 16)
                sp.dma_start(aup[0:64, :], rwkv_a_up[0, :, cs]).then_inc(s_up, 16)
                sp.dma_start(gup[:, 0, :], rwkv_g_up[0, 0:P, cs]).then_inc(s_up, 16)
                sp.dma_start(gup[0:32, 1, :], rwkv_g_up[0, P:, cs]).then_inc(s_up, 16)

            load_up(0)
            for u in range(RING, fill_of[0][0]):
                load(u)
            for g in range(NGRP):
                for u in fill_of[g]:
                    load(u)
                if g + 1 < NGRP:
                    load_up(g + 1)
            load(index["w1k"])
            load(index["w1v"])
            load(index["mem"])
            sp.wait_ge(*dve_rw.at(("out", NGRP - 1)))
            for i, w in enumerate((cmp_w2_k, cmp_w2_v)):
                sp.dma_start(w2[:, i, :], w[0]).then_inc(s_w2, 16)
            for u in range(index["mem"] + 1, loop_first):
                load(u)
            for n, (_, w) in enumerate(LOOPS):
                wv_ = w.rearrange("(c p) n -> p c n", p=P)
                if n == 0:
                    for s in range(2):
                        sp.wait_ge(*freed(loop_first - RING + s))
                        sp.dma_start(unit_kc(s), wv_[:, :, s * UC:s * UC + UC]).then_inc(loop_full[s], 16)
                    sp.wait_ge(*pe_n.at(("na", 3)))
                    sp.dma_start(x, x_in[0].rearrange("(t p) d -> p t d", p=P)).then_inc(s_x, 16)

                def load_looped(i, s):
                    sp.wait_ge(loop_lo, 4 * i + 2 * (NLU * n + s - 1))
                    sp.wait_ge(loop_lo_pool, 4 * i + 2 * (NLU * n + s - 1))
                    sp.dma_start(unit_kc(s), wv_[:, :, bass.ds((2 * i + s) * UC, UC)]).then_inc(loop_full[s], 16)

                if n == 2:
                    load_looped(0, 0)
                    load_looped(0, 1)
                    sp.wait_ge(*pe_m.at(("o", MH - 1)))
                    sp.dma_start(lnb, ln3_g[0].partition_broadcast(P)).then_inc(s_late, 16)
                    sp.dma_start(rw[:, :, 0:NGR], router_group_w[0].rearrange("(p c) n -> p c n", p=P)).then_inc(s_late, 16)
                    sp.dma_start(rw[:, :, NGR:], router_expert_w[0].rearrange("(p c) n -> p c n", p=P)).then_inc(s_late, 16)
                    sp.dma_start(rb[:, 0:NGR], router_group_b[0].partition_broadcast(P)).then_inc(s_late, 16)
                    sp.dma_start(rb[:, NGR:], router_expert_b[0].partition_broadcast(P)).then_inc(s_late, 16)
                with sp.Fori(int(n != 1), NLU // 2) as i:
                    for s in range(2):
                        load_looped(i, s)

            def moe_load(expert, j):
                w = (moe_w_gate, moe_w_up, moe_w_down)[j][0, bass.ds(expert, 1)]
                if j < 2:
                    sp.dma_start(raw[:, j, :].rearrange("p (c n) -> p c n", n=FF),
                                 w.rearrange("e (p c) n -> p (e c) n", p=P)).then_inc(moe_full[j], 16)
                else:
                    sp.dma_start(raw[:, j, :].rearrange("p (c n) -> p c n", n=D),
                                 w.rearrange("e (c p) n -> p (e c) n", p=P)).then_inc(moe_full[j], 16)

            def moe_split(n):
                sp.wait_ge(dve_lo, n)
                sp.wait_ge(pool_lo, n)

            def moe_body(E, gate_up, down):
                moe_split(BH * E)
                moe_load(gate_up, 0)
                moe_split(BH * E + 2)
                moe_load(gate_up, 1)
                moe_split(BH * E + 4)
                moe_load(down, 2)

            sp.wait_ge(pe_loop, NLT)
            for j in range(2):
                moe_load(0, j)
            for j in range(2):
                moe_split(2 + 2 * j)
                moe_load(1, j)
            moe_load(0, 2)
            with sp.Fori(1, NE - 1) as E:
                moe_body(E, E + 1, E)
            sp.wait_ge(*dve_r.at("ovi"))
            nov = sp.value_load(count_i[0:1, 0:1], min_val=0, max_val=1)
            q = sp.value_load(count_i[0:1, 1:2], min_val=0, max_val=NGR - 1)
            last = sp.value_load(count_i[0:1, 2:3], min_val=0, max_val=NGR - 1)
            with sp.If(nov > 0):
                moe_body(NE - 1, q * EPG, NE - 1)
                with sp.Fori(0, EPG - 1) as e:
                    moe_body(e + NE, q * EPG + e + 1, q * EPG + e)
            moe_split(nov * (BH * EPG) + BH * NE - BH + 4)
            moe_load(last * EPG + EPG - 1, 2)
            moe_split(nov * (BH * EPG) + BH * NE)
            sp.dma_start(lnf, lnf_g.partition_broadcast(P)).then_inc(s_late, 16)
            sp.wait_ge(*dve_n.at(("nf", "out")))
            sp.dma_start(out[0].rearrange("(t p) d -> p t d", p=P), x).then_inc(s_out, 16)
            sp.wait_ge(s_out, 16)

        @block.tensor
        def _(pe):
            def project(u, m):
                key = units[u][0]
                b, s, half, c = bank[order[u] % 2], u % RING, m // NC, m % NC
                if m == 0:
                    pe.wait_ge(*full(u))
                    if key in ("misc", "misc2"):
                        pe.wait_ge(s_gl[key == "misc2"], 16)
                    if order[u] >= 2:
                        pe.wait_ge(*act_proj.at(proj[order[u] - 2]))
                    if key == ("mk", 0):
                        pe.wait_ge(*dve_n.at(("nm", "out", 7)))
                w = unit_kc(s)
                st, en = c == 0, c == NC - 1
                if key in TOKMAJOR:
                    mm = pe.matmul(b[:, half * UC:half * UC + UC], hT[:, c, half * P:half * P + P], w[:, c, :],
                                   start=st, stop=en)
                elif key == "misc" and half == 0:
                    mm = pe.matmul(b[:, 0:T], w[:, c, 0:P], hT[:, c, :], start=st, stop=en)
                elif key == "misc":
                    mm = pe.matmul(b[0:64, T:2 * T], w[:, c, P:P + 64], hT[:, c, :], start=st, stop=en)
                elif key == "misc2" and half == 0:
                    mm = pe.matmul(b[0:32, 0:T], w[:, c, 32:64], hT[:, c, :], start=st, stop=en)
                elif key == "misc2":
                    mm = pe.matmul(b[:, T:T + 24], hT[:, c, 0:P], w[:, c, 0:24], start=st, stop=en)
                else:
                    mm = pe.matmul(b[:, half * T:half * T + T], w[:, c, half * P:half * P + P], hT[:, c, :],
                                   start=st, stop=en)
                if m == 2 * NC - 1:
                    if key == "misc":
                        for c in range(NC):
                            mm = pe.matmul(bank[3][0:64, 0:T], w[:, c, P + 64:2 * P], hT[:, c, :],
                                           start=c == 0, stop=c == NC - 1)
                    if key == "misc2":
                        for c in range(NC):
                            mm = pe.matmul(bank[2][:, T:T + 24], hT[:, c, P:2 * P], w[:, c, 0:24],
                                           start=c == 0, stop=c == NC - 1)
                    mm.then_inc(*pe_proj.mark(u))

            def norm_transposes(name, src, nf):
                pe.wait_ge(*dve_n.at((name, "xn")))
                for f in range(nf):
                    tt, c4 = divmod(f, nf // 2)
                    if f >= 4:
                        pe.wait_ge(*dve_n.at((name, "out", f - 4)))
                    for j in range(4):
                        cc = 4 * c4 + j
                        mm = pe.transpose(bank[4 + f % 4][:, j * P:j * P + P], src[:, tt, cc * P:cc * P + P], ident)
                    mm.then_inc(*pe_n.mark((name, f)))

            pe.wait_ge(s_prm, 16 * 18)
            pe.wait_ge(*pool_c.at("ident"))
            pe.transpose(bank[2][:, 0:P], tA[:, 0, 0:P], ident)
            pe.transpose(bank[2][:, P:2 * P], tB[:, 0, 0:P], ident).then_inc(*pe_c.mark("prm"))
            norm_transposes("n1", x_slot, 8)
            pe.wait_ge(*dve_n.at(("n1", "out", 7)))
            for u in range(1, fill_of[0][0]):
                for m in range(2 * NC):
                    project(u, m)
            for g in range(NGRP):
                fl = fill_of[g]
                cur, at = [0], iter(FILLS)

                def gap(n=None):
                    n = next(at) if n is None else n
                    for _ in range(n):
                        if cur[0] < 32 * len(fl):
                            u, m = fl[cur[0] // 32], cur[0] % 32
                            project(u, m)
                            cur[0] += 1

                pe.wait_ge(s_up, 64 * (g + 1))
                if g:
                    pe.wait_ge(*dve_rw.at(("out", g - 1)))
                else:
                    pe.wait_ge(*act_c.at("tm"))
                for pi in range(2):
                    pe.matmul(bank[2][:, pi * T:pi * T + T], wup[0:64, pi * P:pi * P + P], wad[0:64, 0, :],
                              start=True, stop=True)
                for pi in range(2):
                    mm = pe.matmul(bank[3][:, pi * T:pi * T + T], aup[0:64, pi * P:pi * P + P], wad[0:64, 1, :],
                                   start=True, stop=True)
                mm.then_inc(*pe_rw.mark(("wa", g)))
                gap()
                pe.wait_ge(*dve_rw.at(("kx2", g)))
                pe.matmul(bank[4][:, :], bd64, tG.rearrange("p a b -> p (a b)"), start=True, stop=True)\
                  .then_inc(*pe_rw.mark(("ss", g)))
                gap()
                pe.wait_ge(*dve_rw.at(("bon", g)))
                pe.matmul(bank[5][:, :], bd64, tD.rearrange("p a b -> p (a b)"), start=True, stop=True)\
                  .then_inc(*pe_rw.mark(("bon", g)))
                gap()
                pe.wait_ge(*dve_rw.at(("hat", g)))
                for tt in range(NT):
                    for pi in range(2):
                        for j in range(2):
                            pe.transpose(bank[6 + tt][:, (2 * pi + j) * P:(2 * pi + j) * P + P],
                                         BK[:, j, pi, tt * P:tt * P + P], ident)
                for tt in range(NT):
                    for pi in range(2):
                        mm = pe.transpose(bank[2][:, (2 * tt + pi) * P:(2 * tt + pi) * P + P],
                                          z[:, 4 + pi, tt * P:tt * P + P], ident)
                mm.then_inc(*pe_rw.mark(("tr", g)))
                gap()
                for tt in range(NT):
                    if tt == 0:
                        pe.wait_ge(*dve_rw.at(("Vh", g)))
                        pe.wait_ge(*act_rw.at(("trb", g)))
                    else:
                        pe.wait_ge(*dve_rw.at(("G", g, 0)))
                    for j in range(2):
                        for h in range(4):
                            pi, q = divmod(h, 2)
                            mm = pe.matmul(b2(2 + 2 * (1 - j) + pi)[:, q, :].rearrange("p (a b) -> p a b", a=2),
                                           BK[:, j, pi, tt * P:tt * P + P], CR[:, pi, q, :, tt * P:tt * P + P],
                                           start=True, stop=True)
                    for h in range(4):
                        pi, q = divmod(h, 2)
                        mm = pe.matmul(bank[6][:, h * P:h * P + P], CR[:, pi, q, 0, tt * P:tt * P + P],
                                       BK[:, 0, pi, tt * P:tt * P + P], start=True, stop=True)
                    mm.then_inc(*pe_rw.mark(("G", g, tt)))
                    gap()
                for lv in LV:
                    for tt in range(NT):
                        pe.wait_ge(*pool_rw.at(("AM", g, lv, tt)))
                        if lv == 1:
                            pe.wait_ge(*pool_rw.at(("X0", g, tt)))
                            pe.wait_ge(*dve_rw.at(("G", g, 1)))
                        else:
                            pe.wait_ge(*dve_rw.at(("X", g, lv - 1, tt)))
                        for h in range(4):
                            mm = pe.matmul(bank[2 + tt][:, h * P:h * P + P], AM[:, tt, h, :], XI[:, tt, h, :],
                                           start=True, stop=True)
                        mm.then_inc(*pe_rw.mark(("P", g, lv, tt)))
                        gap()
                    for tt in range(NT):
                        pe.wait_ge(*act_rw.at(("Ps", g, lv, tt)))
                        for h in range(4):
                            if lv < 5:
                                pe.matmul(bank[4 + tt][:, h * P:h * P + P], XT[:, tt, h, :], Ps[:, tt, h, :],
                                          start=True, stop=True)
                            mm = pe.matmul(bank[6 + tt][:, h * P:h * P + P], Ps[:, tt, h, :], XT[:, tt, h, :],
                                           start=True, stop=True)
                        mm.then_inc(*pe_rw.mark(("X", g, lv, tt)))
                        gap()
                for c in range(NCH):
                    tt, half = divmod(c, 2)
                    Sc = S[:, c % 2]
                    pe.wait_ge(*(dve_rw.at(("S", g, c - 1)) if c else dve_rw.at(("X", g, 5, 1))))
                    for h in range(4):
                        pi, q = divmod(h, 2)
                        o = bank[2][:, h * CH:h * CH + CH]
                        if c:
                            pe.matmul(o, CR[:, pi, q, 0, tt * P:tt * P + P], Sc[:, pi, :], start=True, stop=False)
                        mm = pe.matmul(o, AK[:, tt, h, 0, :], Vh[:, half, tt, pi, q * CH:q * CH + CH],
                                       start=c == 0, stop=True)
                    mm.then_inc(*pe_rw.mark(("Z", g, c)))
                    gap()
                    pe.wait_ge(*act_rw.at(("Zs", g, c)))
                    for h in range(4):
                        mm = pe.matmul(bank[3][:, h * CH:h * CH + CH], XT[:, tt, h, :], Zs[:, h, :],
                                       start=True, stop=True)
                    mm.then_inc(*pe_rw.mark(("U", g, c)))
                    gap()
                    pe.wait_ge(*dve_rw.at(("Us", g, c)))
                    if c < NCH - 1:
                        for h in range(4):
                            pi, q = divmod(h, 2)
                            o = bank[4][q * CH:q * CH + CH, pi * CH:pi * CH + CH]
                            pe.matmul(o, BKt[:, tt, pi, 0, q * CH:q * CH + CH], Us[:, h, :], start=True, stop=False)
                            pe.matmul(o, BKt[:, tt, pi, 1, q * CH:q * CH + CH],
                                      Vh[:, half, tt, pi, q * CH:q * CH + CH], start=False, stop=True)
                    for h in range(4):
                        pi, q = divmod(h, 2)
                        o = bank[5][q * CH:q * CH + CH, pi * T + c * CH:pi * T + c * CH + CH]
                        pe.matmul(o, Us[:, h, :], AB[:, tt, h, 1, half * CH:half * CH + CH], start=True, stop=False)
                        if c:
                            pe.matmul(o, Sc[:, pi, :], CR[:, pi, q, 1, c * CH:c * CH + CH], start=False, stop=False)
                        mm = pe.matmul(o, Vh[:, half, tt, pi, q * CH:q * CH + CH],
                                       AK[:, tt, h, 1, half * CH:half * CH + CH], start=False, stop=True)
                    mm.then_inc(*pe_rw.mark(("Y", g, c)))
                    gap()
                pe.wait_ge(*act_rw.at(("ys", g)))
                pe.matmul(bank[6][:, :], bd64, tA.rearrange("p a b -> p (a b)"), start=True, stop=True)\
                  .then_inc(*pe_rw.mark(("mean", g)))
                gap()
                pe.wait_ge(*dve_rw.at(("yc", g)))
                if g == 0:
                    pe.wait_ge(*dve_c.at("gds"))
                pe.matmul(bank[7][:, :], bd64, tC.rearrange("p a b -> p (a b)"), start=True, stop=True)
                for pi in range(2):
                    pe.matmul(bank[3][:, pi * T:pi * T + T], gup[:, 0, pi * P:pi * P + P], gds[:, 0, :],
                              start=True, stop=False)
                    mm = pe.matmul(bank[3][:, pi * T:pi * T + T], gup[0:32, 1, pi * P:pi * P + P], gds[0:32, 1, :],
                                   start=False, stop=True)
                mm.then_inc(*pe_rw.mark(("g", g)))
                gap(32 * len(fl))

            pe.wait_ge(*pool_a.at("blk"))
            for i, key in enumerate(("w1k", "w1v")):
                u = index[key]
                pe.wait_ge(*full(u))
                w1 = slot(u % RING).rearrange("p (l f) -> p l f", l=CMP)
                for l in range(CMP):
                    mm = pe.matmul(bank[2 + i][:, 0:2 * NCMP], w1[:, l, :], blk[:, i, l, :],
                                   start=l == 0, stop=l == CMP - 1)
            mm.then_inc(*pe_a.mark("h"))
            norm_transposes("nm", mem_slot, 8)
            pe.wait_ge(*dve_n.at(("nm", "out", 7)))
            pe.wait_ge(*dve_a.at("gelu"))
            pe.wait_ge(s_w2, 32)
            pe.matmul(bank[4][:, 0:2 * NCMP], w2[:, 0, :], hc[:, 0, 0:2 * NCMP], start=True, stop=True)
            for g in range(NG):
                mm = pe.matmul(bank[5][0:NCMP, g * P:g * P + P], hc[:, 1, g * NCMP:g * NCMP + NCMP], w2[:, 1, :],
                               start=True, stop=True)
            mm.then_inc(*pe_a.mark("kv"))

            cur2 = [0]

            def gap2(n):
                for _ in range(n):
                    if cur2[0] < 32 * len(mem_units):
                        u, m = mem_units[cur2[0] // 32], cur2[0] % 32
                        project(u, m)
                        cur2[0] += 1

            def nsa_scores(i):
                h, tt = HT[i]
                nk = P * (tt + 1)
                if i == 0:
                    pe.wait_ge(*dve_a.at("kcmp"))
                if i >= 2:
                    pe.wait_ge(*dve_a.at(("m", i - 2)))
                b = bank[2 + i % 2]
                lhs = qT[:, h, tt * P:tt * P + P]
                for j in range(2):
                    pe.matmul(b[:, j * T:j * T + nk], lhs, ksw[:, 2 * j + h // 4, 0:nk], start=True, stop=True)
                if i:
                    pe.wait_ge(*dve_a.at(("m", i - 1)))
                pe.matmul(bank[4][:, (i % 2) * 16:(i % 2) * 16 + NCMP], lhs,
                          kcmp[:, (h // 4) * NCMP:(h // 4) * NCMP + NCMP], start=True, stop=True)\
                  .then_inc(*pe_a.mark(("s", i)))

            def nsa_transposes(i):
                h, tt = HT[i]
                pe.wait_ge(*dve_a.at(("p", i)))
                if i:
                    pe.wait_ge(*act_a.at(("t", i - 1)))
                p_ = pr[:, i % 2]
                for j in range(2):
                    for kt in range(tt + 1):
                        pe.transpose(bank[5][:, (2 * j + kt) * P:(2 * j + kt) * P + P],
                                     p_[:, j * T + kt * P:j * T + kt * P + P], ident)
                pe.transpose(bank[6][0:NCMP, 0:P], p_[:, 2 * T:2 * T + NCMP], ident).then_inc(*pe_a.mark(("t", i)))

            def nsa_values(i):
                h, tt = HT[i]
                pe.wait_ge(*act_a.at(("t", i)))
                if i:
                    pe.wait_ge(*act_a.at(("o", i - 1)))
                t_ = pT[:, i % 2]
                o = bank[7][:, 0:P]
                n = 0
                for j in range(2):
                    for kt in range(tt + 1):
                        pe.matmul(o, t_[:, 2 * j + kt, :], vsw[:, j, kt, (h // 4) * P:(h // 4) * P + P],
                                  start=n == 0, stop=False)
                        n += 1
                pe.matmul(o, t_[0:NCMP, 4, :], vcmp[0:NCMP, h // 4, :], start=False, stop=True)\
                  .then_inc(*pe_a.mark(("o", i)))

            for i in range(NHT + 2):
                if i < NHT:
                    nsa_scores(i)
                    gap2(FILL2)
                if 0 < i <= NHT:
                    nsa_transposes(i - 1)
                    gap2(FILL2)
                if i > 1:
                    nsa_values(i - 2)
                    gap2(FILL2)
            gap2(32 * len(mem_units))
            norm_transposes("na", ya, 4)
            pe.wait_ge(*act_proj.at(proj[-1]))
            pe.wait_ge(*dve_n.at(("na", "out", 3)))
            pe.nop().then_inc(out_loop, 2)

            PASSES = ((0, 0), (0, 1), (1, 0))

            def looped(n, lhs_tok, src):
                with pe.Fori(0, NLU // 2) as i:
                    for s in range(2):
                        pe.wait_ge(out_loop, n * NLU + s + 1 + 2 * i)
                        for h in range(2):
                            pe.wait_ge(loop_lo, 4 * i + 2 * (NLU * n + s) + h + 1)
                            pe.wait_ge(loop_lo_pool, 4 * i + 2 * (NLU * n + s) + h + 1)
                            for half in range(2):
                                b = bank[2 * s + half][:, 0:UC]
                                for c in range(NC // 2):
                                    cc = NC // 2 * h + c
                                    for k, (x_, y_) in enumerate(PASSES):
                                        flags = dict(start=cc + k == 0, stop=cc == NC - 1 and k == 2)
                                        if lhs_tok:
                                            mm = pe.matmul(b, src[x_][:, cc, half * P:half * P + P],
                                                           lspl[2 * s + h][:, y_, c * UC:c * UC + UC], **flags)
                                        else:
                                            at = c * UC + half * P
                                            mm = pe.matmul(b, lspl[2 * s + h][:, y_, at:at + P], src[x_][:, cc, :],
                                                           **flags)
                        mm.then_inc(pe_loop, 1)

            pe.wait_ge(src_lo, 2)
            looped(0, True, (over_hT, over_concat))
            norm_transposes("n2", xn, 8)
            pe.wait_ge(src_lo, 10)
            looped(1, False, (over_concat, over_hT))

            for h in range(MH):
                for tt in range(NT):
                    if h == 0 and tt == 0:
                        pe.wait_ge(out_loop, 2 + 2 * NLU)
                    if h:
                        pe.wait_ge(*act_m.at(("e", h - 1, tt)))
                    for j in range(4):
                        mm = pe.matmul(bank[2 + tt][:, 0:T], qmT[:, 4 * h + j, tt * P:tt * P + P],
                                       kmT[:, 4 * h + j, :], start=j == 0, stop=j == 3)
                    mm.then_inc(*pe_m.mark(("s", h, tt)))
                pe.wait_ge(*dve_m.at(("p", h, 1)))
                if h:
                    pe.wait_ge(*act_m.at(("t", h - 1)))
                for mt in range(2):
                    for tt in range(NT):
                        mm = pe.transpose(bank[4][:, mt * T + tt * P:mt * T + tt * P + P],
                                          mp[:, tt, mt * P:mt * P + P], ident)
                mm.then_inc(*pe_m.mark(("t", h)))
                pe.wait_ge(*act_m.at(("t", h)))
                if h:
                    pe.wait_ge(src_lo, 10 + h)
                for j in range(4):
                    for mt in range(2):
                        mm = pe.matmul(bank[5 + j // 2][:, (j % 2) * T:(j % 2) * T + T],
                                       vm[:, mt, (4 * h + j) * P:(4 * h + j) * P + P], mpT[:, h % 2, mt, :],
                                       start=mt == 0, stop=mt == 1)
                mm.then_inc(*pe_m.mark(("o", h)))
            pe.wait_ge(src_lo, 10 + MH)
            looped(2, True, (over_concat, over_hT))

            norm_transposes("n3", xn, 8)
            pe.wait_ge(*dve_n.at(("n3", "out", 7)))
            for tt in range(NT):
                for c in range(NC):
                    mm = pe.matmul(bank[2][:, tt * 64:tt * 64 + 36], hT[:, c, tt * P:tt * P + P], rw[:, c, :],
                                   start=c == 0, stop=c == NC - 1)
            mm.then_inc(*pe_r.mark("logits"))
            pe.wait_ge(*dve_r.at("routed"))
            pe.matmul(bank[3][:, 0:NGR], strictU, goh[:, 0, :], start=True, stop=True)
            pe.matmul(bank[3][:, 64:64 + NGR], ones, goh[:, 0, :], start=True, stop=False)
            pe.matmul(bank[3][:, 64:64 + NGR], strictU, goh[:, 1, :], start=False, stop=True)\
              .then_inc(*pe_r.mark("pos"))
            for tt in range(NT):
                mm = pe.matmul(bank[2][:, 128:128 + NGR], ones, goh[:, tt, :], start=tt == 0, stop=tt == 1)
            mm.then_inc(*pe_r.mark("cnt"))

            def gather(n, again):
                pe.wait_ge(pool_g, n + 1)
                if again:
                    pe.wait_ge(dve_gt, n)
                for tt in range(NT):
                    mm = pe.matmul(bank[0][:, 0:EPG], G[:, tt, :].bitcast(F32), ccol[:, tt, :],
                                   start=tt == 0, stop=tt == 1)
                mm.then_inc(pe_cm, 1)
                for f in range(4):
                    if f >= 2:
                        pe.wait_ge(dve_hs, 4 * n + f - 1)
                    for j in range(4):
                        c = 4 * f + j
                        for tt in range(NT):
                            for part in range(2):
                                mm = pe.matmul(bank[3 - f % 2][:, j * P:j * P + P], h3[part][:, tt, c * P:c * P + P],
                                               G[:, tt, :], start=tt + part == 0, stop=tt + part == 2)
                    mm.then_inc(pe_hs, 1)
                pe.wait_ge(dve_hs, 4 * n + 4)

            def onehots(n, again):
                if again:
                    pe.wait_ge(dve_sc, 8 * n)
                for tt in range(NT):
                    mm = pe.transpose(bank[3][:, tt * P:tt * P + P], G[:, tt, :].bitcast(F32), ident)
                mm.then_inc(pe_gt, 1)

            def scatter(m):
                for f in range(8):
                    q, tt = divmod(f, 2)
                    if tt == 0:
                        pe.wait_ge(dve_os, 4 * m + q + 1)
                    if f >= 2:
                        pe.wait_ge(dve_sc, 8 * m + f - 1)
                    for part in range(2):
                        mm = pe.matmul(bank[3 - f % 2][:, :], Gt[:, tt, :], osp[q % 2][:, part, :],
                                       start=part == 0, stop=part == 1)
                    mm.then_inc(pe_sc, 1)

            def split_ready(E, off):
                n = half_unit(E, off)
                pe.wait_ge(dve_lo, n + 1)
                pe.wait_ge(pool_lo, n + 1)

            def gate_up(E, off, parity):
                split_ready(E, off)
                j, hf = divmod(off, 2)
                sl = spl[(off if E is None else 4 + off) % SPLITS]
                for c in range(NC // 2):
                    for k, (a, b) in enumerate(PASSES):
                        mm = pe.matmul(bank[parity][:, j * FF:j * FF + FF], hs[a][:, NC // 2 * hf + c, :],
                                       sl[:, b, c * FF:c * FF + FF], start=hf + c + k == 0,
                                       stop=hf == 1 and c == NC // 2 - 1 and k == 2)
                mm.then_inc(pe_hu, 1)

            def hidden_transposes(E):
                pe.wait_ge(dve_hid, E + 1)
                for j in range(2):
                    mm = pe.transpose(bank[2][:, j * P:j * P + P], hid[:, j * P:j * P + P], ident)
                mm.then_inc(pe_trh, 1)

            def down(E, start, stop, tail=False):
                pe.wait_ge(dve_tT, E + 1)
                for f in range(2):
                    off = f if tail else 4 + f
                    split_ready(E, off)
                    sl = spl[(4 + off) % SPLITS]
                    for q in range(4):
                        for k, (a, b) in enumerate(PASSES):
                            mm = pe.matmul(bank[4 + q][:, :], tTs[a][:, f, :], sl[:, b, q * 512:q * 512 + 512],
                                           start=start and f + k == 0, stop=stop and f + k == 3)
                    mm.then_inc(pe_hu, 1)

            def body(E, parity, start=False, stop=False):
                gate_up(E, 0, parity)
                gate_up(E, 1, parity)
                hidden_transposes(E)
                gate_up(E, 2, parity)
                gate_up(E, 3, parity)
                down(E, start, stop)

            def bodies(n):
                body(n * EPG, 1, start=True)
                with pe.Fori(0, EPG // 2 - 1) as j:
                    for k in range(2):
                        body(n * EPG + 2 * j + 1 + k, k)

            def group(n):
                gather(n, True)
                body(n * EPG - 1, 0, stop=True)
                scatter(n - 1)
                onehots(n, True)
                bodies(n)

            pe.wait_ge(*dve_r.at("most"))
            pe.wait_ge(*dve_r.at("h3lo"))
            gather(0, False)
            for off in range(4):
                gate_up(None, off, 0)
            onehots(0, False)
            bodies(0)
            with pe.Fori(1, NGR) as n:
                group(n)
            pe.wait_ge(*dve_r.at("ovi"))
            nov = pe.value_load(count_i[0:1, 0:1], min_val=0, max_val=1)
            with pe.If(nov > 0):
                group(NGR)
            last = nov * EPG + (NE - 1)
            hidden_transposes(last)
            down(last, False, True, tail=True)
            scatter(nov + (NGR - 1))

        @block.scalar
        def _(act):
            act_self_ = Chain(act, act_self)
            A = nc.scalar.activation

            def sumsq(name, src, n, junk):
                for tt in range(NT):
                    ins = A(junk, src[:, tt, 0:n], ACT.Square, accum_out=rms_s[:, tt:tt + 1])
                    if tt == 0:
                        act_self_(ins)
                ins.then_inc(*act_n.mark((name, "sq")))
                act.wait_ge(*dve_n.at((name, "var")))
                A(rms_s, rms_r, ACT.Sqrt).then_inc(*act_n.mark((name, "sqrt")))

            def copy_out(u):
                key = units[u][0]
                act.wait_ge(*pe_proj.at(u))
                i = order[u] % 2
                if key == "misc":
                    nc.scalar.copy(zraw[:, 0, 1:T + 1], bank[i][:, 0:T])
                    nc.scalar.copy(zraw[0:64, 1, 1:T + 1], bank[i][0:64, T:2 * T])
                    ins = nc.scalar.copy(zraw[0:64, 2, 1:T + 1], bank[3][0:64, 0:T])
                elif key == "misc2":
                    nc.scalar.copy(zraw[0:32, 3, 1:T + 1], bank[i][0:32, 0:T])
                    A(gates[:, 0, :], bank[i][:, T:T + 24], ACT.Tanh, scale=0.5)
                    ins = A(gates[:, 1, :], bank[2][:, T:T + 24], ACT.Tanh, scale=0.5)
                elif key[0] == "rkv":
                    act.wait_ge(*(dve_rw.at(("mix", key[1] - 1)) if key[1] else dve_c.at("mixm")))
                    ins = nc.scalar.copy(zraw[:, 2 * key[2]:2 * key[2] + 2, 1:T + 1], b2(i))
                else:
                    j = key[1]
                    if key[0] == "mv":
                        dst = vm[:, :, j * UC:j * UC + UC]
                    elif key[0] in ("vs", "vw"):
                        dst = vsw[:, ("vs", "vw").index(key[0])]
                    else:
                        into, at = {"q": (qT, 2 * j), "mk": (kmT, 2 * j), "kc": (kvc, 0), "vc": (kvc, 2),
                                    "ks": (ksw, 0), "kw": (ksw, 2)}[key[0]]
                        dst = into[:, at:at + 2, :]
                    ins = nc.scalar.copy(dst, b2(i))
                ins.then_inc(*act_proj.mark(u))

            act.wait_ge(*full(0))
            sumsq("n1", x_slot, D, flat(hT)[:, 0:D])
            act.wait_ge(*pool_c.at("masks"))
            first = list(range(1, fill_of[0][0]))
            copy_out(first[0])
            copy_out(first[1])
            act.wait_ge(*dve_c.at("mixm"))
            A(wad[0:64, 0, :], z[0:64, 1, :], ACT.Tanh)
            A(gds[:, 0, :], z[:, 0, :], ACT.Tanh, scale=0.5)
            A(gds[0:32, 1, :], z[0:32, 3, :], ACT.Tanh, scale=0.5).then_inc(*act_c.mark("tm"))
            for u in first[2:]:
                copy_out(u)

            for g in range(NGRP):
                fl = fill_of[g]
                cur, at = [0], iter(FILLS)

                def gap(n=None):
                    n = next(at) if n is None else n
                    old, cur[0] = cur[0], min(cur[0] + n, 32 * len(fl))
                    for j in range(old // 32, cur[0] // 32):
                        copy_out(fl[j])

                act.wait_ge(*pe_rw.at(("wa", g)))
                for pi in range(2):
                    cw, ca = 2 * g + pi, 8 + 2 * g + pi
                    A(tA[:, pi, :], b2(2)[:, pi, :], ACT.Tanh, bias=prm2[:, cw:cw + 1], scale=0.5)
                    ins = A(tB[:, pi, :], b2(3)[:, pi, :], ACT.Tanh, bias=prm2[:, ca:ca + 1], scale=0.5)
                ins.then_inc(*act_rw.mark(("th", g)))
                gap()
                act.wait_ge(*dve_rw.at(("D", g)))
                A(flat(tE), flat(tD), ACT.Exp, scale=-KAPPA)
                A(flat(tH), flat(tD), ACT.Exp, scale=KAPPA)
                A(flat(tA), flat(tA), ACT.Exp, scale=-KAPPA)
                A(em, tC.rearrange("p a (c t) -> p a c t", t=CH)[:, :, :, CH // 2 - 1], ACT.Exp, scale=-KAPPA)\
                    .then_inc(*act_rw.mark(("exp", g)))
                act.wait_ge(*dve_rw.at(("ssm", g)))
                A(flat(tG), flat(tG), ACT.Sqrt).then_inc(*act_rw.mark(("sq1", g)))
                gap()
                gap()
                act.wait_ge(*pe_rw.at(("tr", g)))
                for tt in range(NT):
                    ins = nc.scalar.copy(BKt[:, tt].rearrange("p a b c -> p (a b c)"), bank[6 + tt][:, :])
                ins.then_inc(*act_rw.mark(("trb", g)))
                gap()
                gap()
                gap()
                for lv in LV:
                    for tt in range(NT):
                        act.wait_ge(*pe_rw.at(("P", g, lv, tt)))
                        nc.scalar.copy(flat(Ps[:, tt]), bank[2 + tt][:, :]).then_inc(*act_rw.mark(("Ps", g, lv, tt)))
                        gap()
                    gap()
                    gap()
                for c in range(NCH):
                    act.wait_ge(*pe_rw.at(("Z", g, c)))
                    nc.scalar.copy(flat(Zs), bank[2][:, 0:T]).then_inc(*act_rw.mark(("Zs", g, c)))
                    gap()
                    gap()
                    if c < NCH - 1:
                        gap()
                act.wait_ge(*pe_rw.at(("Y", g, NCH - 1)))
                nc.scalar.copy(flat(tA), bank[5][:, :]).then_inc(*act_rw.mark(("ys", g)))
                gap()
                gap()
                act.wait_ge(*dve_rw.at(("ve", g)))
                A(flat(tG), flat(tG), ACT.Sqrt).then_inc(*act_rw.mark(("sq2", g)))
                gap(32 * len(fl))

            act.wait_ge(*dve_rw.at(("out", NGRP - 1)))
            act.wait_ge(*full(index["mem"]))
            sumsq("nm", mem_slot, D, flat(kmT)[:, 0:D])
            act.wait_ge(*pe_a.at("h"))
            for i in range(2):
                ins = nc.scalar.copy(hc[:, i, 0:2 * NCMP], bank[2 + i][:, 0:2 * NCMP])
            ins.then_inc(*act_a.mark("hc"))
            act.wait_ge(*dve_a.at("cube"))
            A(hc3[:, :, 0:2 * NCMP], hc2[:, :, 0:2 * NCMP], ACT.Tanh, scale=0.7978845608028654)\
                .then_inc(*act_a.mark("th"))

            cur2 = [0]

            def gap2(n):
                old, cur2[0] = cur2[0], min(cur2[0] + n, 32 * len(mem_units))
                for j in range(old // 32, cur2[0] // 32):
                    copy_out(mem_units[j])

            SC = HD ** -0.5
            for i in range(NHT + 2):
                if i < NHT:
                    h, tt = HT[i]
                    nk = P * (tt + 1)
                    act.wait_ge(*dve_a.at(("m", i)))
                    if i >= 2:
                        act.wait_ge(*pe_a.at(("t", i - 2)))
                    p_, s_, m_, a_ = pr[:, i % 2], sm[:, i % 2], mxs[:, i % 2], sums[:, i % 2]
                    A(p_[:, 2 * T:2 * T + NCMP], s_[:, 2 * T:2 * T + NCMP], ACT.Exp, bias=m_[:, 0:1], scale=SC)
                    for j in range(2):
                        ins = A(p_[:, j * T:j * T + nk], s_[:, j * T:j * T + nk], ACT.Exp, bias=m_[:, 1 + j:2 + j],
                                scale=SC, accum_out=a_[:, 1 + j:2 + j])
                    ins.then_inc(*act_a.mark(("e", i)))
                    gap2(FILL2)
                if 0 < i <= NHT:
                    h, tt = HT[i - 1]
                    nk = P * (tt + 1)
                    act.wait_ge(*pe_a.at(("t", i - 1)))
                    if i >= 3:
                        act.wait_ge(*pe_a.at(("o", i - 3)))
                    t_ = pT[:, (i - 1) % 2]
                    nc.scalar.copy(flat(t_[:, 0:4]).rearrange("p (a b) -> p a b", a=2)[:, :, 0:nk], b2(5)[:, :, 0:nk])
                    nc.scalar.copy(t_[0:NCMP, 4, :], bank[6][0:NCMP, 0:P]).then_inc(*act_a.mark(("t", i - 1)))
                    gap2(FILL2)
                if i > 1:
                    h, tt = HT[i - 2]
                    act.wait_ge(*pe_a.at(("o", i - 2)))
                    nc.scalar.copy(ya[:, tt, h * P:h * P + P], bank[7][:, 0:P]).then_inc(*act_a.mark(("o", i - 2)))
                    gap2(FILL2)
            gap2(32 * len(mem_units))
            act.wait_ge(*act_a.at(("o", NHT - 1)))
            def activations_hi(dst, src, c0, c1):
                nc.scalar.copy(dst[:, c0:c1, :], src[:, c0:c1, :]).then_inc(src_hi, 1)

            def loop_weights(at, s):
                act.wait_ge(loop_full[s], 8 * at + 16)
                for h in range(2):
                    nc.scalar.copy(lspl[2 * s + h][:, 0, :], slot(s)[:, h * HU:h * HU + HU]).then_inc(loop_hi, 1)

            def loop_stream(n, out_copy=False, last=False):
                def step(i, s, weights):
                    act.wait_ge(pe_loop, 2 * i + n * NLU + s + 1)
                    if out_copy:
                        for half in range(2):
                            ins = nc.scalar.copy(qmT[:, bass.ds(4 * i + 2 * s + half, 1), :],
                                                 bank[2 * s + half][:, 0:UC].unsqueeze(1))
                        ins.then_inc(out_loop, 1)
                    if weights:
                        loop_weights(2 * i + n * NLU + 2, s)

                with act.Fori(0, NLU // 2 - int(last)) as i:
                    for s in range(2):
                        step(i, s, True)

            activations_hi(over_hT, concatT, NC // 2, NC)
            sumsq("na", ya, NH * HD, pr.rearrange("p a b -> p (a b)")[:, 0:NH * HD])
            loop_weights(0, 0)
            act.wait_ge(*dve_n.at(("na", "out", 3)))
            activations_hi(over_hT, concatT, 0, NC // 2)
            loop_weights(0, 1)
            loop_stream(0)
            act.wait_ge(out_loop, 2 + NLU)
            sumsq("n2", x, D, flat(hT)[:, 0:D])
            for f in range(8):
                tt, c4 = divmod(f, 4)
                act.wait_ge(*dve_n.at(("n2", "out", f)))
                o = (slice(None), slice(4 * c4, 4 * c4 + 4), slice(tt * P, tt * P + P))
                nc.scalar.copy(over_concat[o], hT[o]).then_inc(src_hi, 1)
            loop_stream(1, out_copy=True)
            for h in range(MH):
                for tt in range(NT):
                    act.wait_ge(*dve_m.at(("m", h, tt)))
                    if h:
                        act.wait_ge(*pe_m.at(("t", h - 1)))
                    A(mp[:, tt, :], bank[2 + tt][:, 0:T], ACT.Exp, bias=mst[:, tt, 1:2], scale=MHD ** -0.5,
                      accum_out=mst[:, tt, 2:3]).then_inc(*act_m.mark(("e", h, tt)))
                act.wait_ge(*pe_m.at(("t", h)))
                nc.scalar.copy(flat(mpT[:, h % 2]), bank[4][:, :]).then_inc(*act_m.mark(("t", h)))
                act.wait_ge(*pe_m.at(("o", h)))
                for j in range(2):
                    ins = nc.scalar.copy(over_concat[:, 4 * h + 2 * j:4 * h + 2 * j + 2, :], b2(5 + j))
                ins.then_inc(*act_m.mark(("o", h)))
            loop_stream(2, last=True)
            act.wait_ge(out_loop, 2 + 3 * NLU)
            sumsq("n3", x, D, flat(hT)[:, 0:D])
            act.wait_ge(*dve_n.at(("n3", "xn")))
            nc.scalar.copy(h3[0][:, :, :], xn).then_inc(*act_r.mark("h3hi"))
            act.wait_ge(*dve_r.at("gd"))
            A(ge, gd_, ACT.Exp).then_inc(*act_r.mark("ge"))
            act.wait_ge(*dve_r.at("m2"))
            A(e2, m2, ACT.Exp).then_inc(*act_r.mark("e2"))

            def gathered(n):
                for f in range(4):
                    act.wait_ge(pe_hs, 4 * n + f + 1)
                    nc.scalar.copy(hs[0][:, 4 * f:4 * f + 4, :], b2(3 - f % 2, 4)).then_inc(act_hs, 1)

            def weights(E, off, tail=False):
                n = half_unit(E, off)
                j, hf = divmod(off + 4 * tail, 2)
                if hf == 0:
                    act.wait_ge(moe_full[j], 16 * loads_of(E, off + 4 * tail))
                if E is not None or off >= SPLITS:
                    act.wait_ge(pe_hu, n + 1 - SPLITS)
                sl = spl[(off if E is None else 4 + off) % SPLITS]
                nc.scalar.copy(sl[:, 0, :], raw[:, j, hf * HU:hf * HU + HU]).then_inc(act_hi, 1)

            def tanh(E, parity, done):
                act.wait_ge(pe_hu, done)
                A(thm, bank[parity][:, 0:FF], ACT.Tanh, scale=0.5).then_inc(act_th, 1)

            def hidden(E):
                act.wait_ge(pe_trh, E + 1)
                nc.scalar.copy(tTs[0][:, :, :], b2(2, 4)[:, 0:2, :]).then_inc(act_tT, 1)

            def down(m, q, done):
                if q < 2:
                    act.wait_ge(pe_hu, done)
                else:
                    act.wait_ge(pe_sc, 8 * m + 2 * q - 2)
                nc.scalar.copy(osp[q % 2][:, 0, :], bank[4 + q][:, :]).then_inc(act_os, 1)

            def body(E, parity, first=0):
                for off in range(first, 4):
                    weights(E, off)
                hidden(E)
                weights(E, 4)
                weights(E, 5)
                tanh(E + 1, parity, half_unit(E, 4))

            def bodies(n, first):
                body(n * EPG, 1, first)
                with act.Fori(0, EPG // 2 - 1) as j:
                    for k in range(2):
                        body(n * EPG + 2 * j + 1 + k, k)

            def group(n):
                weights(n * EPG - 1, 0)
                weights(n * EPG - 1, 1)
                gathered(n)
                body(n * EPG - 1, 0, first=2)
                weights(n * EPG, 0)
                weights(n * EPG, 1)
                done = half_unit(n * EPG - 1, BH)
                down(n - 1, 0, done)
                down(n - 1, 1, done)
                weights(n * EPG, 2)
                down(n - 1, 2, done)
                down(n - 1, 3, done)
                bodies(n, 3)

            gathered(0)
            for off in range(4):
                weights(None, off)
            tanh(0, 0, 4)
            bodies(0, 0)
            with act.Fori(1, NGR) as n:
                group(n)
            act.wait_ge(*dve_r.at("ovi"))
            nov = act.value_load(count_i[0:1, 0:1], min_val=0, max_val=1)
            with act.If(nov > 0):
                group(NGR)
            last = nov * EPG + (NE - 1)
            weights(last, 0, tail=True)
            hidden(last)
            weights(last, 1, tail=True)
            for q in range(4):
                down(nov + (NGR - 1), q, half_unit(last, 2))
            act.wait_ge(dve_sc, nov * 8 + 8 * NGR)
            sumsq("nf", x, D, slot(1)[:, 0:D])

        @block.vector
        def _(dve):
            link = Chain(dve, dve_self)
            V = nc.vector

            def norm(name, src, dst, n, gain=None, order=lambda ap: ap):
                dve.wait_ge(*act_n.at((name, "sq")))
                V.tensor_scalar(rms_r, rms_s, 1.0 / n, EPS, ALU.mult, ALU.add).then_inc(*dve_n.mark((name, "var")))
                dve.wait_ge(*act_n.at((name, "sqrt")))
                link(V.reciprocal(rms_r, rms_s))
                for tt in range(NT):
                    if gain is None:
                        ins = V.tensor_scalar(dst[:, tt, 0:n], src[:, tt, 0:n], rms_r[:, tt:tt + 1], None, ALU.mult)
                    else:
                        o = dst[:, tt, 0:n]
                        if order is by_partition:
                            o = o.rearrange("q (c p) -> q c p", p=P)
                        ins = V.scalar_tensor_tensor(out=o, in0=order(src[:, tt, 0:n]), scalar=rms_r[:, tt:tt + 1],
                                                     in1=order(gain), op0=ALU.mult, op1=ALU.mult)
                return ins

            def by_partition(ap):
                return ap.rearrange("q (p c) -> q c p", c=NC)

            def norm_out(name, dst, gcol, then=None):
                nf = fills[name]
                for f in range(nf):
                    tt, c4 = divmod(f, nf // 2)
                    dve.wait_ge(*pe_n.at((name, f)))
                    o = dst[:, 4 * c4:4 * c4 + 4, tt * P:tt * P + P]
                    if gcol is None:
                        ins = V.tensor_copy(o, b2(4 + f % 4, 4))
                    else:
                        g_ = prm[:, gcol + 4 * c4:gcol + 4 * c4 + 4].unsqueeze(2)
                        ins = V.tensor_tensor(o, b2(4 + f % 4, 4), bc(g_, 4, P), ALU.mult)
                    ins.then_inc(*dve_n.mark((name, "out", f)))
                    if then and f:
                        then(f - 1)
                if then:
                    then(nf - 1)

            dve.wait_ge(*pe_c.at("prm"))
            link(V.tensor_copy(prm, bank[2][:, 0:2 * P]))
            V.tensor_scalar(prm2[:, 0:16], prm[:, c_w0:c_w0 + 16], 0.5, None, ALU.mult)
            link(V.tensor_scalar(prm2[:, 16:24], prm[:, c_ka:c_ka + 8], -1.0, 1.0, ALU.mult, ALU.add))
            V.tensor_copy(prm2[:, 24:25], prm2[:, 23:24])\
                .then_inc(*dve_c.mark("prm"))
            norm("n1", x_slot, x_slot, D).then_inc(*dve_n.mark(("n1", "xn")))
            norm_out("n1", hT, c_ln1)

            def shift_mix(dst, i, n, rows, mucol, tmp):
                link(V.tensor_tensor(tmp[0:rows, 0:n], zraw[0:rows, i:i + n, 0:T], zraw[0:rows, i:i + n, 1:T + 1],
                                     ALU.subtract))
                for j in range(n):
                    ins = V.scalar_tensor_tensor(out=dst[j], in0=tmp[0:rows, j, :], scalar=prm[0:rows, mucol + j:mucol + j + 1],
                                                 in1=zraw[0:rows, i + j, 1:T + 1], op0=ALU.mult, op1=ALU.add)
                return ins

            dve.wait_ge(*act_proj.at(index["misc2"]))
            link(shift_mix([z[:, 0, :]], 0, 1, P, c_mu + 26, tC))
            link(shift_mix([z[0:64, 1, :]], 1, 1, 64, c_mu + 24, tC))
            link(shift_mix([wad[0:64, 1, :]], 2, 1, 64, c_mu + 25, tC))
            link(V.tensor_scalar(gates, gates, 0.5, 0.5, ALU.mult, ALU.add))
            shift_mix([z[0:32, 3, :]], 3, 1, 32, c_mu + 27, tC).then_inc(*dve_c.mark("mixm"))
            dve.wait_ge(*act_c.at("tm"))
            V.tensor_scalar(gds[0:32, 1, :], gds[0:32, 1, :], 0.5, 0.5, ALU.mult, ALU.add)
            V.tensor_scalar(gds[:, 0, :], gds[:, 0, :], 0.5, 0.5, ALU.mult, ALU.add).then_inc(*dve_c.mark("gds"))
            dve.wait_ge(*pool_c.at("masks"))

            for g in range(NGRP):
                for j in range(3):
                    dve.wait_ge(*act_proj.at(index[("rkv", g, j)]))
                    ins = shift_mix([z[:, 2 * j + t, :] for t in range(2)], 2 * j, 2, P, c_mu + 8 * j + 2 * g, tC)
                    if j < 2:
                        link(ins)
                ins.then_inc(*dve_rw.mark(("mix", g)))
                dve.wait_ge(*dve_rw.at(("mix", g)))
                zr, zk, zv = z[:, 0:2, :], z[:, 2:4, :], z[:, 4:6, :]
                for pi in range(2):
                    ins = V.tensor_scalar(tF[:, pi, :], zk[:, pi, :], col(c_kk + 2 * g + pi), None, ALU.mult)
                link(ins)
                V.tensor_tensor(tG, tF, tF, ALU.mult).then_inc(*dve_rw.mark(("kx2", g)))
                dve.wait_ge(*act_rw.at(("th", g)))
                V.tensor_scalar(flat(tB), flat(tB), 0.5, 0.5, ALU.mult, ALU.add)
                link(V.tensor_scalar(flat(tA), flat(tA), 0.5, 0.5, ALU.mult, ALU.add))
                for pi in range(2):
                    ins = V.tensor_tensor_scan(tC[:, pi, :], reset, tA[:, pi, :], 0.0, ALU.mult, ALU.add)
                link(ins)
                C4 = tC.rearrange("p a (c t) -> p (a c) t", t=CH)
                link(V.tensor_tensor(tD.rearrange("p a (c t) -> p (a c) t", t=CH), C4,
                                     bc(C4[:, :, CH // 2 - 1:CH // 2], 8, CH), ALU.subtract))
                V.tensor_tensor(tA, tD, tA, ALU.subtract).then_inc(*dve_rw.mark(("D", g)))
                dve.wait_ge(*pe_rw.at(("ss", g)))
                V.tensor_scalar(flat(tG), bank[4][:, :], 1e-24, None, ALU.max).then_inc(*dve_rw.mark(("ssm", g)))
                dve.wait_ge(*act_rw.at(("sq1", g)))
                link(V.reciprocal(flat(tG), flat(tG)))
                link(V.tensor_tensor(tF, tF, tG, ALU.mult))
                for pi in range(2):
                    ins = V.tensor_scalar(tG[:, pi, :], tB[:, pi, :], col(c_ka + 2 * g + pi),
                                          prm2[:, 16 + 2 * g + pi:17 + 2 * g + pi], ALU.mult, ALU.add)
                link(ins)
                link(V.tensor_tensor(tG, tG, zk, ALU.mult))
                for pi in range(2):
                    ins = V.scalar_tensor_tensor(out=tD[:, pi, :], in0=zr[:, pi, :], scalar=col(c_rk + 2 * g + pi),
                                                 in1=tG[:, pi, :], op0=ALU.mult, op1=ALU.mult)
                ins.then_inc(*dve_rw.mark(("bon", g)))
                for q in range(2):
                    V.scalar_tensor_tensor(out=CR[:, :, q, 0, :], in0=tF, scalar=hm[:, 2 + q:3 + q], in1=tA,
                                           op0=ALU.mult, op1=ALU.mult)
                    V.scalar_tensor_tensor(out=CR[:, :, q, 1, :], in0=zr, scalar=hm[:, q:q + 1], in1=tE,
                                           op0=ALU.mult, op1=ALU.mult)
                link(V.tensor_tensor(tB, tF, tB, ALU.mult))
                V.tensor_tensor(BK[:, 0], tB, tH, ALU.mult)
                V.tensor_tensor(BK[:, 1], tG, tH, ALU.mult)
                V.tensor_tensor(fac[:, :, 0:NCH - 1], tE.rearrange("p a (c t) -> p a c t", t=CH)[:, :, 0:NCH - 1, CH - 1],
                                em[:, :, 1:NCH], ALU.mult).then_inc(*dve_rw.mark(("hat", g)))
                dve.wait_ge(*pe_rw.at(("bon", g)))
                V.tensor_tensor(tI, b2(5), zv, ALU.mult)
                dve.wait_ge(*pe_rw.at(("tr", g)))
                for half in range(2):
                    ins = V.tensor_scalar(Vh[:, half].rearrange("p a b c -> p (a b c)"), bank[2][:, :],
                                          hm[:, half:half + 1], None, ALU.mult)
                ins.then_inc(*dve_rw.mark(("Vh", g)))
                m2_ = bc(flat(M2).unsqueeze(1), 2, 2 * P)
                for tt in range(NT):
                    dve.wait_ge(*pe_rw.at(("G", g, tt)))
                    for pi in range(2):
                        for dst, b in ((AK, 2 + pi), (AB, 4 + pi)):
                            V.tensor_tensor(dst[:, tt, 2 * pi:2 * pi + 2].rearrange("p a b c -> p a (b c)"), b2(b),
                                            m2_, ALU.mult)
                    link(V.tensor_tensor(XI[:, tt], b2(6, 4), bc(M0.unsqueeze(1), 4, P), ALU.mult))
                    V.tensor_tensor(XI[:, tt], XI[:, tt], bc(ident.unsqueeze(1), 4, P), ALU.add)\
                        .then_inc(*dve_rw.mark(("G", g, tt)))
                dve.wait_ge(*dve_rw.at(("G", g, 1)))
                for lv in LV:
                    for tt in range(NT):
                        dve.wait_ge(*pe_rw.at(("X", g, lv, tt)))
                        if lv > 1:
                            dve.wait_ge(*dve_rw.at(("X", g, lv - 1, tt)))
                        else:
                            dve.wait_ge(*pool_rw.at(("X0", g, tt)))
                        if lv < 5:
                            V.tensor_tensor(XI[:, tt], XI[:, tt], b2(4 + tt, 4), ALU.add)
                        V.tensor_tensor(XT[:, tt], XT[:, tt], b2(6 + tt, 4), ALU.add)\
                            .then_inc(*dve_rw.mark(("X", g, lv, tt)))
                for c in range(NCH):
                    dve.wait_ge(*pe_rw.at(("U", g, c)))
                    V.tensor_scalar(flat(Us), bank[3][:, 0:T], hm[:, c % 2:c % 2 + 1], None, ALU.mult)\
                        .then_inc(*dve_rw.mark(("Us", g, c)))
                    if c < NCH - 1:
                        dve.wait_ge(*pe_rw.at(("Y", g, c)))
                        Pc = bank[4][:, 0:2 * CH].rearrange("p (a b) -> p a b", a=2)
                        f_ = bc(fac[:, :, c:c + 1], 2, CH)
                        if c:
                            dve.wait_ge(*dve_rw.at(("S", g, c - 1)))
                            link(V.tensor_tensor(S[:, c % 2], S[:, c % 2], Pc, ALU.add))
                        V.tensor_tensor(S[:, (c + 1) % 2], S[:, c % 2] if c else Pc, f_, ALU.mult)\
                            .then_inc(*dve_rw.mark(("S", g, c)))
                dve.wait_ge(*pe_rw.at(("mean", g)))
                link(V.scalar_tensor_tensor(out=flat(tB), in0=bank[6][:, :], scalar=-1.0 / CH, in1=flat(tA),
                                            op0=ALU.mult, op1=ALU.add))
                V.tensor_tensor(tC, tB, tB, ALU.mult).then_inc(*dve_rw.mark(("yc", g)))
                dve.wait_ge(*pe_rw.at(("g", g)))
                V.tensor_scalar(flat(tG), bank[7][:, :], 1.0 / CH, LNX_EPS, ALU.mult, ALU.add)\
                    .then_inc(*dve_rw.mark(("ve", g)))
                dve.wait_ge(*act_rw.at(("sq2", g)))
                link(V.reciprocal(flat(tG), flat(tG)))
                link(V.tensor_tensor(tB, tB, tG, ALU.mult))
                for pi in range(2):
                    ins = V.tensor_scalar(tB[:, pi, :], tB[:, pi, :], col(c_lg + 2 * g + pi), col(c_lb + 2 * g + pi),
                                          ALU.mult, ALU.add)
                link(ins)
                link(V.tensor_tensor(tB, tB, tI, ALU.add))
                V.tensor_tensor(concatT[:, 8 + 2 * g:10 + 2 * g, :], tB, b2(3), ALU.mult)\
                    .then_inc(*dve_rw.mark(("out", g)))

            norm("nm", mem_slot, mem_slot, D).then_inc(*dve_n.mark(("nm", "xn")))
            dve.wait_ge(*act_proj.at(last_in))
            hcv, hc2v, hc3v = (t[:, :, 0:2 * NCMP] for t in (hc, hc2, hc3))
            dve.wait_ge(*act_a.at("hc"))
            link(V.tensor_tensor(hc2v, hcv, hcv, ALU.mult))
            link(V.tensor_scalar(hc2v, hc2v, 0.044715, 1.0, ALU.mult, ALU.add))
            V.tensor_tensor(hc2v, hc2v, hcv, ALU.mult).then_inc(*dve_a.mark("cube"))
            norm_out("nm", hT, c_lnm)
            dve.wait_ge(*act_a.at("th"))
            link(V.scalar_tensor_tensor(out=hcv, in0=hc3v, scalar=1.0, in1=hcv, op0=ALU.add, op1=ALU.mult))
            V.tensor_scalar(hcv, hcv, 0.5, None, ALU.mult).then_inc(*dve_a.mark("gelu"))
            dve.wait_ge(*pe_a.at("kv"))
            V.tensor_copy(kcmp[:, 0:2 * NCMP], bank[4][:, 0:2 * NCMP])
            V.tensor_copy(flat(vcmp)[0:NCMP], bank[5][0:NCMP, 0:2 * P]).then_inc(*dve_a.mark("kcmp"))
            SC = HD ** -0.5
            dve.wait_ge(*pool_c.at("nsa"))
            for i in range(NHT + 1):
                if i < NHT:
                    h, tt = HT[i]
                    nk = P * (tt + 1)
                    s_, m_ = sm[:, i % 2], mxs[:, i % 2]
                    s2 = s_[:, 0:2 * T].rearrange("p (a b) -> p a b", a=2)[:, :, 0:nk]
                    dve.wait_ge(*pe_a.at(("s", i)))
                    if i >= 2:
                        dve.wait_ge(*act_a.at(("e", i - 2)))
                    V.tensor_tensor(s2, b2(2 + i % 2)[:, :, 0:nk], bc(biasw[:, tt, 0:nk].unsqueeze(1), 2, nk), ALU.add)
                    link(V.tensor_tensor(s_[:, 2 * T:2 * T + NCMP], bank[4][:, (i % 2) * 16:(i % 2) * 16 + NCMP],
                                         biasc[:, tt, 0:NCMP], ALU.add))
                    V.tensor_reduce(m_[:, 0:1], s_[:, 2 * T:2 * T + NCMP], AX.X, ALU.max)
                    link(V.tensor_reduce(m_[:, 1:3], s2, AX.X, ALU.max))
                    V.tensor_scalar(m_[:, 0:3], m_[:, 0:3], -SC, None, ALU.mult).then_inc(*dve_a.mark(("m", i)))
                if i > 0:
                    h, tt = HT[i - 1]
                    nk = P * (tt + 1)
                    b = (i - 1) % 2
                    p_, a_, c_ = pr[:, b], sums[:, b], coef[:, b]
                    pc = p_[:, 2 * T:2 * T + NCMP]
                    dve.wait_ge(*act_a.at(("e", i - 1)))
                    link(V.tensor_tensor(pc, pc, maskc[:, tt, 0:NCMP], ALU.mult))
                    link(V.tensor_reduce(a_[:, 0:1], pc, AX.X, ALU.add))
                    link(V.tensor_scalar(c_[:, 0:3], a_[:, 0:3], 1e-30, None, ALU.max))
                    link(V.reciprocal(c_[:, 0:3], c_[:, 0:3]))
                    link(V.tensor_tensor(c_[:, 0:3], c_[:, 0:3],
                                         gates[:, tt].rearrange("p (b h) -> p b h", b=3)[:, :, h], ALU.mult))
                    V.tensor_scalar(pc, pc, c_[:, 0:1], None, ALU.mult)
                    p2 = p_[:, 0:2 * T].rearrange("p (a b) -> p a b", a=2)[:, :, 0:nk]
                    V.tensor_tensor(p2, p2, bc(c_[:, 1:3].unsqueeze(2), 2, nk), ALU.mult)\
                        .then_inc(*dve_a.mark(("p", i - 1)))
            def activations_lo(dst, src, hi, o, count):
                dve.wait_ge(src_hi, count)
                V.tensor_tensor(dst[o], src[o], hi[o].bitcast(F32), ALU.subtract).then_inc(src_lo, 1)

            def loop_weights(at, s):
                for h in range(2):
                    dve.wait_ge(loop_hi, 2 * at + 2 * s + h + 1)
                    sl = lspl[2 * s + h]
                    V.tensor_tensor(sl[:, 1, 0:DSHARE], slot(s)[:, h * HU:h * HU + DSHARE],
                                    sl[:, 0, 0:DSHARE].bitcast(F32), ALU.subtract).then_inc(loop_lo, 1)

            everything = slice(None)
            activations_lo(over_concat, concatT, over_hT, (everything, slice(NC // 2, NC), everything), 1)
            norm("na", ya, ya, NH * HD).then_inc(*dve_n.mark(("na", "xn")))
            norm_out("na", concatT, c_nsa)

            loop_weights(0, 0)
            activations_lo(over_concat, concatT, over_hT, (everything, slice(0, NC // 2), everything), 2)
            loop_weights(0, 1)

            def loop_stream(n, residual=True, last=False):
                def step(i, s, weights):
                    if residual:
                        dve.wait_ge(pe_loop, 2 * i + n * NLU + s + 1)
                        for tt in range(NT):
                            xs = x[:, tt, bass.ds((2 * i + s) * UC, UC)]
                            ins = V.tensor_tensor(xs, xs, bank[2 * s + tt][:, 0:UC], ALU.add)
                        ins.then_inc(out_loop, 1)
                    if weights:
                        loop_weights(2 * i + n * NLU + 2, s)

                with dve.Fori(0, NLU // 2 - int(last)) as i:
                    for s in range(2):
                        step(i, s, True)
                if last:
                    for s in range(2):
                        step(NLU // 2 - 1, s, False)

            dve.wait_ge(s_x, 16)
            loop_stream(0)
            norm("n2", x, xn, D).then_inc(*dve_n.mark(("n2", "xn")))

            def split_n2(f):
                tt, c4 = divmod(f, 4)
                o = (everything, slice(4 * c4, 4 * c4 + 4), slice(tt * P, tt * P + P))
                activations_lo(over_hT, hT, over_concat, o, 3 + f)

            norm_out("n2", hT, c_ln2, then=split_n2)
            loop_stream(1, residual=False)

            def output_lo(h):
                dve.wait_ge(*act_m.at(("o", h)))
                for j in range(2):
                    o = (everything, slice(4 * h + 2 * j, 4 * h + 2 * j + 2), everything)
                    ins = V.tensor_tensor(over_hT[o], b2(5 + j), over_concat[o].bitcast(F32), ALU.subtract)
                ins.then_inc(src_lo, 1)

            for h in range(MH):
                for tt in range(NT):
                    dve.wait_ge(*pe_m.at(("s", h, tt)))
                    link(V.tensor_reduce(mst[:, tt, 0:1], bank[2 + tt][:, 0:T], AX.X, ALU.max))
                    V.tensor_scalar(mst[:, tt, 1:2], mst[:, tt, 0:1], -MHD ** -0.5, None, ALU.mult)\
                        .then_inc(*dve_m.mark(("m", h, tt)))
                for tt in range(NT):
                    dve.wait_ge(*act_m.at(("e", h, tt)))
                    link(V.reciprocal(mst[:, tt, 3:4], mst[:, tt, 2:3]))
                    V.tensor_scalar(mp[:, tt, :], mp[:, tt, :], mst[:, tt, 3:4], None, ALU.mult)\
                        .then_inc(*dve_m.mark(("p", h, tt)))
                if h:
                    output_lo(h - 1)
            output_lo(MH - 1)
            loop_stream(2, last=True)
            dve.wait_ge(s_late, 80)
            norm("n3", x, xn, D, gain=lnb, order=by_partition).then_inc(*dve_n.mark(("n3", "xn")))
            norm_out("n3", hT, None)
            dve.wait_ge(*act_r.at("h3hi"))
            V.tensor_tensor(h3[1][:, :, :], xn, h3[0][:, :, :].bitcast(F32), ALU.subtract).then_inc(*dve_r.mark("h3lo"))

            dve.wait_ge(*pool_c.at("moe"))
            dve.wait_ge(*pe_r.at("logits"))
            TT = V.tensor_tensor

            def first_only(dst, eq, w):
                n = w.shape[-1]
                link(TT(dst, eq, bc(w.unsqueeze(1), 2, n), ALU.mult))
                link(V.tensor_reduce(rtop, dst, AX.X, ALU.max))
                link(TT(dst, dst, bc(rtop.unsqueeze(2), 2, n), ALU.is_equal))

            link(TT(lg, bank[2][:, 0:2 * 64].rearrange("p (a b) -> p a b", a=2)[:, :, 0:36],
                    bc(rb.unsqueeze(1), 2, 36), ALU.add))
            link(V.tensor_reduce(rmax, lg[:, :, 0:NGR], AX.X, ALU.max))
            TT(gd_, lg[:, :, 0:NGR], bc(rmax.unsqueeze(2), 2, NGR), ALU.subtract).then_inc(*dve_r.mark("gd"))
            dve.wait_ge(*act_r.at("ge"))
            link(V.tensor_reduce(pg, ge, AX.X, ALU.add))
            link(V.reciprocal(pg, pg))
            link(V.tensor_scalar(geq, gd_, 0.0, None, ALU.is_equal))
            first_only(goh, geq, wtie[:, 0:NGR])
            lge = lg[:, :, NGR:].rearrange("p t (g j) -> p t j g", g=NGR)
            tmp = rtmp.rearrange("p t (j g) -> p t j g", g=NGR)
            link(TT(tmp, lge, bc(goh.unsqueeze(2), 2, EPG, NGR), ALU.mult))
            link(V.tensor_reduce(d8, tmp, AX.X, ALU.add))
            link(V.tensor_reduce(rmax, d8, AX.X, ALU.max))
            link(TT(d8, d8, bc(rmax.unsqueeze(2), 2, EPG), ALU.subtract))
            link(V.tensor_scalar(eq8, d8, 0.0, None, ALU.is_equal))
            first_only(o1, eq8, wtie)
            link(V.scalar_tensor_tensor(out=flat(d8), in0=flat(o1), scalar=BIG, in1=flat(d8), op0=ALU.mult, op1=ALU.add))
            V.tensor_reduce(m2, d8, AX.X, ALU.max).then_inc(*dve_r.mark("m2"))
            dve.wait_ge(*act_r.at("e2"))
            link(TT(eq8, d8, bc(m2.unsqueeze(2), 2, EPG), ALU.is_equal))
            first_only(o2, eq8, wtie)
            link(V.tensor_scalar(w1_, e2, 1.0, None, ALU.add))
            link(V.reciprocal(w1_, w1_))
            link(TT(w1_, w1_, pg, ALU.mult))
            link(TT(w2_, w1_, e2, ALU.mult))
            link(V.tensor_scalar(w1_, w1_, 0.5, None, ALU.mult))
            link(V.tensor_scalar(w2_, w2_, 0.5, None, ALU.mult))
            link(TT(c8, o1, bc(w1_.unsqueeze(2), 2, EPG), ALU.mult))
            link(TT(eq8, o2, bc(w2_.unsqueeze(2), 2, EPG), ALU.mult))
            link(TT(c8, c8, eq8, ALU.add))
            link(TT(o1, o1, o2, ALU.add))
            for t in range(NT):
                g4 = bc(goh[:, t].unsqueeze(2), NGR, EPG)
                ins = TT(comb[:, t, 0:NE].rearrange("p (g j) -> p g j", g=NGR), g4, bc(c8[:, t].unsqueeze(1), NGR, EPG),
                         ALU.mult)
            ins.then_inc(*dve_r.mark("routed"))
            dve.wait_ge(*dve_r.at("routed"))
            dve.wait_ge(*pe_r.at("pos"))
            pg_ = posm[:, :, 0:NGR]
            link(V.scalar_tensor_tensor(out=pg_, in0=bank[3][:, 0:2 * 64].rearrange("p (a b) -> p a b", a=2)[:, :, 0:NGR],
                                        scalar=1.0, in1=goh, op0=ALU.add, op1=ALU.mult))
            link(V.tensor_scalar(pg_, pg_, -1.0, None, ALU.add))
            V.tensor_copy(otmp[:, 0:2], posm[:, 0, 0:2]).then_inc(*dve_r.mark("posm"))
            dve.wait_ge(*pe_r.at("cnt"))
            V.tensor_scalar(oflag, bank[2][:, 128:128 + NGR], float(CAP), None, ALU.is_gt)\
                .then_inc(*dve_r.mark("most"))
            dve.wait_ge(*dve_r.at("most"))
            link(TT(geq, pg_, bc(oflag.unsqueeze(1), 2, NGR), ALU.mult))
            link(V.tensor_reduce(rtop, geq, AX.X, ALU.add))
            link(V.tensor_scalar(posm[:, :, NGR:].rearrange("p t o -> p (t o)"), rtop, -float(CAP), None, ALU.add))
            o4 = bc(oflag.unsqueeze(1).unsqueeze(1), 2, EPG, NGR)
            link(TT(tmp, comb[:, :, 0:NE].rearrange("p t (g j) -> p t j g", g=NGR), o4, ALU.mult))
            link(V.tensor_reduce(comb[:, :, NE:], tmp, AX.X, ALU.add))
            link(TT(otmp4, oflag, kval, ALU.mult))
            link(V.tensor_reduce(osum[:, 0:1], oflag, AX.X, ALU.add))
            link(V.tensor_reduce(osum[:, 1:2], otmp4, AX.X, ALU.add))
            link(V.scalar_tensor_tensor(out=osum[:, 2:3], in0=osum[:, 0:1], scalar=-(NGR - 1.0), in1=osum[:, 1:2],
                                        op0=ALU.mult, op1=ALU.add))
            link(V.tensor_scalar(osum[:, 2:3], osum[:, 2:3], NGR - 1.0, None, ALU.add))
            V.tensor_copy(count_i[:, 0:3], osum).then_inc(*dve_r.mark("ovi"))

            def weights(E, off, tail=False):
                j, hf = divmod(off + 4 * tail, 2)
                r = raw[:, j, hf * HU:hf * HU + DSHARE]
                sl = spl[(off if E is None else 4 + off) % SPLITS]
                dve.wait_ge(act_hi, half_unit(E, off) + 1)
                V.tensor_tensor(sl[:, 1, 0:DSHARE], r, sl[:, 0, 0:DSHARE].bitcast(F32), ALU.subtract)\
                    .then_inc(dve_lo, 1)

            def down(m, q):
                dve.wait_ge(act_os, 4 * m + q + 1)
                o = osp[q % 2]
                V.tensor_tensor(o[:, 1, :], bank[4 + q][:, :], o[:, 0, :].bitcast(F32), ALU.subtract).then_inc(dve_os, 1)

            def add(m, f):
                q, tt = divmod(f, 2)
                dve.wait_ge(pe_sc, 8 * m + f + 1)
                xs = x[:, tt, q * 512:q * 512 + 512]
                V.tensor_tensor(xs, xs, bank[3 - f % 2][:, :], ALU.add).then_inc(dve_sc, 1)

            def gathered(n):
                dve.wait_ge(pe_cm, n + 1)
                V.tensor_copy(wcol, bank[0][:, 0:EPG])
                for f in range(4):
                    dve.wait_ge(act_hs, 4 * n + f + 1)
                    o = slice(4 * f, 4 * f + 4)
                    V.tensor_tensor(hs[1][:, o, :], b2(3 - f % 2, 4), hs[0][:, o, :].bitcast(F32), ALU.subtract)\
                        .then_inc(dve_hs, 1)

            def onehots(n):
                dve.wait_ge(pe_gt, n + 1)
                V.tensor_copy(Gt[:, :, :], b2(3, 4)[:, 0:2, :]).then_inc(dve_gt, 1)

            def hidden_values(E, parity, e):
                dve.wait_ge(act_th, E + 1)
                V.tensor_copy(wc1, wcol[:, bass.ds(e, 1)])
                V.scalar_tensor_tensor(out=hid, in0=thm, scalar=1.0, in1=bank[parity][:, 0:FF], op0=ALU.add,
                                       op1=ALU.mult).then_inc(dve_h1, 1)
                dve.wait_ge(dve_h1, E + 1)
                V.scalar_tensor_tensor(out=hid, in0=hid, scalar=wc1, in1=bank[parity][:, FF:2 * FF], op0=ALU.mult,
                                       op1=ALU.mult).then_inc(dve_hid, 1)

            def hidden(E):
                dve.wait_ge(act_tT, E + 1)
                V.tensor_tensor(tTs[1][:, :, :], b2(2, 4)[:, 0:2, :], tTs[0][:, :, :].bitcast(F32), ALU.subtract)\
                    .then_inc(dve_tT, 1)

            def body(E, parity, e, first=0):
                for off in range(first, 4):
                    weights(E, off)
                hidden(E)
                weights(E, 4)
                weights(E, 5)
                hidden_values(E + 1, parity, e)

            def bodies(n, first):
                body(n * EPG, 1, 1, first)
                with dve.Fori(0, EPG // 2 - 1) as j:
                    for k in range(2):
                        body(n * EPG + 2 * j + 1 + k, k, 2 * j + 2 + k)

            def group(n):
                weights(n * EPG - 1, 0)
                weights(n * EPG - 1, 1)
                gathered(n)
                body(n * EPG - 1, 0, 0, first=2)
                weights(n * EPG, 0)
                weights(n * EPG, 1)
                down(n - 1, 0)
                down(n - 1, 1)
                weights(n * EPG, 2)
                for f in range(8):
                    add(n - 1, f)
                    if f in (1, 3):
                        down(n - 1, 2 + f // 2)
                onehots(n)
                bodies(n, 3)

            gathered(0)
            for off in range(4):
                weights(None, off)
            onehots(0)
            hidden_values(0, 0, 0)
            bodies(0, 0)
            with dve.Fori(1, NGR) as n:
                group(n)
            nov = dve.value_load(count_i[0:1, 0:1], min_val=0, max_val=1)
            with dve.If(nov > 0):
                group(NGR)
            last = nov * EPG + (NE - 1)
            weights(last, 0, tail=True)
            hidden(last)
            weights(last, 1, tail=True)
            last_group = nov + (NGR - 1)
            down(last_group, 0)
            down(last_group, 1)
            for f in range(8):
                add(last_group, f)
                if f in (1, 3):
                    down(last_group, 2 + f // 2)
            dve.wait_ge(s_late, 96)
            norm("nf", x, x, D, gain=lnf).then_inc(*dve_n.mark(("nf", "out")))

        @block.gpsimd
        def _(pool):
            link = Chain(pool, pool_self)
            G_ = nc.gpsimd

            def select(ap, op, base, pattern, ch, fill=0.0):
                return G_.affine_select(out=ap, in_=ap, compare_op=op, fill=fill, base=base, pattern=pattern,
                                        channel_multiplier=ch)

            G_.memset(tA[:, 0, 0:P], 0.0)
            G_.memset(tB[:, 0, 0:P], 0.0).then_inc(*pool_c.mark("clear"))
            link(G_.memset(ident, 0.0))
            link(select(ident, ALU.not_equal, 0, [[-1, P]], 1, fill=1.0))
            G_.memset(zraw, 0.0).then_inc(*pool_c.mark("ident"))
            bds = {}
            for k, B in enumerate((2, 4, 8, 16, 32, 64)):
                m = bd64 if B == CH else MTk[:, k, :]
                link(G_.memset(m, 1.0))
                v = m.rearrange("p (n b) -> p n b", b=B)
                link(select(v, ALU.is_ge, 0, [[-B, P // B], [0, B]], 1))
                link(select(v, ALU.is_ge, B - 1, [[B, P // B], [0, B]], -1))
                bds[B] = m
            for j in range(2):
                link(G_.tensor_copy(M2[:, j, :], bd64))
                link(select(M2[:, j, :], ALU.is_gt if j == 0 else ALU.is_ge, 0, [[1, P]], -1))
            link(G_.tensor_copy(M0, bds[2]))
            link(select(M0, ALU.is_gt, 0, [[-1, P]], 1))
            link(G_.tensor_copy(MTk[:, 5, :], bd64))
            for k in range(5, 0, -1):
                link(G_.tensor_tensor(MTk[:, k, :], MTk[:, k, :], MTk[:, k - 1, :], ALU.subtract))
            for k in range(6):
                link(select(MTk[:, k, :], ALU.is_gt, 0, [[1, P]], -1))
            link(G_.memset(reset, 1.0))
            rv = reset.rearrange("p (c t) -> p c t", t=CH)
            link(select(rv, ALU.not_equal, 0, [[0, NCH], [1, CH]], 0))
            for j in range(2):
                v = hm[:, 2 * j:2 * j + 2]
                link(G_.memset(v, 1.0 - 2 * j))
                link(select(hm[:, 2 * j:2 * j + 1], ALU.is_ge, CH - 1, [[0, 1]], -1))
                link(select(hm[:, 2 * j + 1:2 * j + 2], ALU.is_ge, -CH, [[0, 1]], 1))
            for tt in range(NT):
                link(G_.memset(maskc[:, tt, :], 1.0))
                link(select(maskc[:, tt, :], ALU.is_ge, tt * P - CMP + 1, [[-STRIDE, 16]], 1))
                link(G_.memset(biasc[:, tt, :], 0.0))
                link(select(biasc[:, tt, :], ALU.is_ge, tt * P - CMP + 1, [[-STRIDE, 16]], 1, fill=BIG))
            G_.tensor_copy(maskc[:, 0, 15:16], maskc[:, 0, 15:16]).then_inc(*pool_c.mark("masks"))

            for g in range(NGRP):
                for tt in range(NT):
                    pool.wait_ge(*dve_rw.at(("G", g, tt)))
                    link(G_.tensor_tensor(XT[:, tt], AB[:, tt, :, 0, :], bc(MTk[:, 0, :].unsqueeze(1), 4, P), ALU.mult))
                    G_.tensor_tensor(XT[:, tt], XT[:, tt], bc(ident.unsqueeze(1), 4, P), ALU.add)\
                        .then_inc(*pool_rw.mark(("X0", g, tt)))
                for lv in LV:
                    for tt in range(NT):
                        if lv > 1:
                            pool.wait_ge(*pe_rw.at(("P", g, lv - 1, tt)))
                        G_.tensor_tensor(AM[:, tt], AB[:, tt, :, 0, :], bc(MTk[:, lv, :].unsqueeze(1), 4, P), ALU.mult)\
                            .then_inc(*pool_rw.mark(("AM", g, lv, tt)))

            pool.wait_ge(*dve_rw.at(("out", NGRP - 1)))
            pool.wait_ge(*act_proj.at(last_in))
            for i in range(2):
                for g in range(NG):
                    kv = kvc[:, 2 * i + g, :].rearrange("p (m r) -> p m r", r=STRIDE)
                    for lh in range(2):
                        o = blk[:, i, lh * 16:lh * 16 + 16, g * NCMP:g * NCMP + NCMP].rearrange("p l c -> p c l")
                        c0 = (c_posk, c_posv)[i] + lh * 16
                        ins = G_.tensor_tensor(o, kv[:, lh:lh + NCMP, :], bc(prm[:, c0:c0 + 16].unsqueeze(1), NCMP, 16),
                                               ALU.add)
            ins.then_inc(*pool_a.mark("blk"))
            for tt in range(NT):
                link(G_.memset(biasw[:, tt, :], 0.0))
                link(select(biasw[:, tt, :], ALU.is_ge, tt * P, [[-1, T]], 1, fill=BIG))
            G_.tensor_copy(biasw[:, 0, 0:1], biasw[:, 0, 0:1]).then_inc(*pool_c.mark("nsa"))

            with pool.Fori(0, NLT // 2) as i:
                for s in range(2):
                    for h in range(2):
                        pool.wait_ge(loop_hi, 4 * i + 2 * s + h + 1)
                        sl = lspl[2 * s + h]
                        G_.tensor_tensor(sl[:, 1, DSHARE:HU], slot(s)[:, h * HU + DSHARE:h * HU + HU],
                                         sl[:, 0, DSHARE:HU].bitcast(F32), ALU.subtract).then_inc(loop_lo_pool, 1)

            pool.wait_ge(pe_loop, NLT)
            iota = G_.iota
            link(iota(ioti[:, 0:CAP], [[1, CAP]], base=0, channel_multiplier=0))
            link(G_.tensor_copy(iota_r, ioti[:, 0:CAP]))
            link(iota(ioti[:, 0:8], [[-1, 8]], base=8, channel_multiplier=0))
            link(G_.tensor_copy(wtie, ioti[:, 0:8]))
            link(iota(ioti[:, 0:NGR], [[1, NGR]], base=0, channel_multiplier=0))
            link(G_.tensor_copy(kval, ioti[:, 0:NGR]))
            link(G_.memset(ones, 1.0))
            link(G_.memset(strictU, 1.0))
            select(strictU, ALU.is_gt, 0, [[1, P]], -1).then_inc(*pool_c.mark("moe"))
            pool.wait_ge(*dve_r.at("posm"))

            def carry(k):
                G_.tensor_tensor(otick[:, k:k + 1], ones[:, 0:1], ones[:, 0:1], ALU.mult)

            def onehots(n):
                if n is None:
                    G_.tensor_copy(ccol, comb[:, :, 0:EPG])
                    G_.tensor_copy(pcol, posm[:, :, 0:1]).then_inc(pool_mc, 1)
                    pool.wait_ge(pool_mc, 1)
                else:
                    pool.wait_ge(pe_gt, n)
                    carry(0)
                    G_.tensor_copy(ccol, comb[:, :, bass.ds(n * EPG, EPG)])
                    G_.tensor_copy(pcol, posm[:, :, bass.ds(n, 1)]).then_inc(pool_mc, 1)
                    pool.wait_ge(pool_mc, n + 1)
                    carry(1)
                for tt in range(NT):
                    ins = G_.tensor_scalar(G[:, tt, :], iota_r, pcol[:, tt, :], None, ALU.is_equal)
                ins.then_inc(pool_g, 1)

            def weights(E, off, tail=False):
                j, hf = divmod(off + 4 * tail, 2)
                r = raw[:, j, hf * HU + DSHARE:hf * HU + HU]
                sl = spl[(off if E is None else 4 + off) % SPLITS]
                pool.wait_ge(act_hi, half_unit(E, off) + 1)
                G_.tensor_tensor(sl[:, 1, DSHARE:HU], r, sl[:, 0, DSHARE:HU].bitcast(F32), ALU.subtract)\
                    .then_inc(pool_lo, 1)

            def body(E):
                for off in range(BH):
                    weights(E, off)

            onehots(None)
            pool.wait_ge(*dve_r.at("ovi"))
            for off in range(4):
                weights(None, off)
            body(0)
            onehots(1)
            with pool.Fori(1, EPG - 1) as E:
                body(E)
            with pool.Fori(1, NGR) as n:
                body(n * EPG - 1)
                body(n * EPG)
                onehots(n + 1)
                with pool.Fori(1, EPG - 1) as e:
                    body(n * EPG + e)
            nov = pool.value_load(count_i[0:1, 0:1], min_val=0, max_val=1)
            with pool.If(nov > 0):
                with pool.Fori(NE - 1, NE + EPG - 1) as E:
                    body(E)
            last = nov * EPG + (NE - 1)
            for off in range(2):
                weights(last, off, tail=True)


_INS = ["x", "mem", "ln1_g", "w_in", "cmp_pos_k", "cmp_w1_k", "cmp_w2_k", "cmp_pos_v", "cmp_w1_v", "cmp_w2_v",
        "nsa_norm_g", "rwkv_mu", "rwkv_w0", "rwkv_w_up", "rwkv_a0", "rwkv_a_up", "rwkv_g_up", "rwkv_k_k",
        "rwkv_k_a", "rwkv_r_k", "rwkv_lnx_g", "rwkv_lnx_b", "w_out", "ln_mem_g", "ln2_g", "wq_mem", "wk_mem",
        "wv_mem", "wo_mem", "ln3_g", "router_group_w", "router_group_b", "router_expert_w", "router_expert_b",
        "moe_w_gate", "moe_w_up", "moe_w_down", "lnf_g"]
_OUTS = [((1, T, D), "float32")]


def kernel(**inputs):
    import numpy as _np
    import concourse.bacc as _bacc
    from concourse import mybir as _mybir
    from concourse.bass_utils import run_bass_kernel_spmd as _run

    nc = _bacc.Bacc("TRN2", target_bir_lowering=False, num_devices=1)
    arrays, args = {}, []
    for name in _INS:
        a = _np.ascontiguousarray(inputs[name])
        arrays[f"in_{name}_dram"] = a
        args.append(nc.dram_tensor(f"in_{name}_dram", a.shape, _mybir.dt.from_np(a.dtype), kind="ExternalInput").ap())
    for i, (shape, dtype) in enumerate(_OUTS):
        dt = _mybir.dt.from_np(_np.dtype(dtype))
        args.append(nc.dram_tensor(f"out_{i}_dram", shape, dt, kind="ExternalOutput").ap())
    decoder_layer(nc, *args)
    r = _run(nc, [arrays], core_ids=[0])
    got = tuple(r.results[0][f"out_{i}_dram"] for i in range(len(_OUTS)))
    return got[0]
```
